# Optimizing a Trainium2 kernel written in Bass

```python
import math
import jax, jax.numpy as jnp
from jax import lax
import numpy as np

D_MODEL = 1024
BATCH = 1
SEQ = 512
DEPTH = 1

CHUNK = 64
Q_BLOCK = 128

DSA_WIDTH = D_MODEL // 2
DSA_HEAD_DIM = 64
DSA_HEADS = DSA_WIDTH // DSA_HEAD_DIM
IDX_HEADS = 8
IDX_DIM = 64
TOPK_MAX = 256

HG_WIDTH = D_MODEL - DSA_WIDTH
HG_DK = 128
HG_HEADS = HG_WIDTH // HG_DK
HG_DV = HG_WIDTH // HG_HEADS

D_FF = ((8 * D_MODEL // 3 + 255) // 256) * 256

ALPHA = (2.0 * DEPTH) ** 0.25
BETA = (8.0 * DEPTH) ** -0.25
LN_EPS = 1e-5
RMS_EPS = 1e-6

SPLIT_SIZES = (DSA_WIDTH, DSA_WIDTH, DSA_WIDTH, IDX_HEADS * IDX_DIM, IDX_DIM, IDX_HEADS,
               HG_HEADS * HG_DK, HG_HEADS * HG_DK, HG_WIDTH, HG_WIDTH)
D_PROJ = sum(SPLIT_SIZES)

kernel_name = "hybrid_dsa_hgrn2_deepnorm_block"

def _split_points():
    pts, acc = [], 0
    for s in SPLIT_SIZES[:-1]:
        acc += s
        pts.append(acc)
    return pts

def _layer_norm(x, g, b):
    xf = x.astype(jnp.float32)
    mu = jnp.mean(xf, axis=-1, keepdims=True)
    var = jnp.mean(jnp.square(xf - mu), axis=-1, keepdims=True)
    y = (xf - mu) * lax.rsqrt(var + LN_EPS) * g.astype(jnp.float32) + b.astype(jnp.float32)
    return y.astype(x.dtype)

def _alibi_slopes(n):
    return 2.0 ** (-8.0 * jnp.arange(1, n + 1, dtype=jnp.float32) / n)

def _dsa_attention(q, k, v, iq, ik, iw):
    B, S = q.shape[0], q.shape[1]
    topk = min(TOPK_MAX, S // 4)
    n_blk = S // Q_BLOCK
    slopes = _alibi_slopes(DSA_HEADS)
    key_pos = jnp.arange(S, dtype=jnp.int32)
    scale = DSA_HEAD_DIM ** -0.5
    idx_scale = (IDX_DIM ** -0.5) * (IDX_HEADS ** -0.5)
    gather = jax.vmap(lambda t, i: t[i])

    def block(bi):
        start = bi * Q_BLOCK
        qb = lax.dynamic_slice_in_dim(q, start, Q_BLOCK, axis=1)
        iqb = lax.dynamic_slice_in_dim(iq, start, Q_BLOCK, axis=1)
        iwb = lax.dynamic_slice_in_dim(iw, start, Q_BLOCK, axis=1)
        qpos = start + jnp.arange(Q_BLOCK, dtype=jnp.int32)
        limit = (qpos // CHUNK + 1) * CHUNK
        adm = key_pos[None, :] < limit[:, None]
        rel = jax.nn.relu(jnp.einsum('bqhd,bsd->bqhs', iqb, ik).astype(jnp.float32))
        score = jnp.einsum('bqh,bqhs->bqs', iwb.astype(jnp.float32), rel) * idx_scale
        score = jnp.where(adm[None], score, -jnp.inf)
        _, sel = lax.top_k(score, topk)
        kg = gather(k, sel)
        vg = gather(v, sel)
        logits = jnp.einsum('bqhd,bqkhd->bhqk', qb, kg).astype(jnp.float32) * scale
        dist = jnp.abs(qpos[None, :, None] - sel).astype(jnp.float32)
        logits = logits - slopes[None, :, None, None] * dist[:, None]
        valid = sel < limit[None, :, None]
        logits = jnp.where(valid[:, None], logits, -jnp.inf)
        p = jax.nn.softmax(logits, axis=-1).astype(v.dtype)
        return jnp.einsum('bhqk,bqkhd->bqhd', p, vg)

    out = lax.map(block, jnp.arange(n_blk))
    return out.transpose(1, 0, 2, 3, 4).reshape(B, S, DSA_HEADS * DSA_HEAD_DIM)

def _hgrn2(q, f_logit, inp, lb):
    f32 = jnp.float32
    B, S, H, Dk = q.shape
    Dv = inp.shape[-1]
    nc = S // CHUNK
    f = lb + (1.0 - lb) * jax.nn.sigmoid(f_logit.astype(f32))
    logf = jnp.log(f)
    kk = 1.0 - f

    def to_chunks(t):
        return t.reshape(B, nc, CHUNK, t.shape[2], t.shape[3]).transpose(1, 0, 3, 2, 4)

    tri = jnp.tril(jnp.ones((CHUNK, CHUNK), dtype=bool))

    def step(state, xs):
        qc, lfc, kc, vc = xs
        G = jnp.cumsum(lfc, axis=2)
        diff = G[:, :, :, None, :] - G[:, :, None, :, :]
        decay = jnp.exp(jnp.where(tri[:, :, None], diff, -jnp.inf))
        A = jnp.einsum('bhtk,bhtsk,bhsk->bhts', qc, decay, kc)
        o = jnp.einsum('bhts,bhsv->bhtv', A, vc) + \
            jnp.einsum('bhtk,bhkv->bhtv', qc * jnp.exp(G), state)
        G_last = G[:, :, -1:, :]
        state = jnp.exp(G_last[:, :, 0])[..., None] * state + \
            jnp.einsum('bhsk,bhsv->bhkv', kc * jnp.exp(G_last - G), vc)
        return state, o

    s0 = jnp.zeros((B, H, Dk, Dv), f32)
    _, o = lax.scan(step, s0, (to_chunks(q.astype(f32)), to_chunks(logf),
                               to_chunks(kk), to_chunks(inp.astype(f32))))
    return o.transpose(1, 0, 3, 2, 4).reshape(B, S, H, Dv)

def setup_inputs(seed: int = 0) -> dict:
    key = jax.random.key(seed)
    keys = jax.random.split(key, 16)
    f32 = jnp.float32
    x = jax.random.normal(keys[0], (BATCH, SEQ, D_MODEL), f32)
    col_scale = []
    for j, s in enumerate(SPLIT_SIZES):
        col_scale.append(jnp.full((s,), BETA if j in (2, 8) else 1.0, f32))
    col_scale = jnp.concatenate(col_scale)
    w_in = jax.random.normal(keys[1], (DEPTH, D_MODEL, D_PROJ), f32) * (D_MODEL ** -0.5) * col_scale
    w_out = jax.random.normal(keys[2], (DEPTH, D_MODEL, D_MODEL), f32) * (D_MODEL ** -0.5) * BETA
    hg_lb_logits = 0.1 * jax.random.normal(keys[3], (DEPTH + 1, HG_HEADS * HG_DK), f32)
    hg_norm_g = 1.0 + 0.02 * jax.random.normal(keys[4], (DEPTH, HG_WIDTH), f32)
    ln1_g = 1.0 + 0.02 * jax.random.normal(keys[5], (DEPTH, D_MODEL), f32)
    ln1_b = 0.02 * jax.random.normal(keys[6], (DEPTH, D_MODEL), f32)
    w_gate = jax.random.normal(keys[7], (DEPTH, D_MODEL, D_FF), f32) * (D_MODEL ** -0.5) * BETA
    w_up = jax.random.normal(keys[8], (DEPTH, D_MODEL, D_FF), f32) * (D_MODEL ** -0.5) * BETA
    w_down = jax.random.normal(keys[9], (DEPTH, D_FF, D_MODEL), f32) * (D_FF ** -0.5) * BETA
    ln2_g = 1.0 + 0.02 * jax.random.normal(keys[10], (DEPTH, D_MODEL), f32)
    ln2_b = 0.02 * jax.random.normal(keys[11], (DEPTH, D_MODEL), f32)
    return {"x": x, "w_in": w_in, "w_out": w_out, "hg_lb_logits": hg_lb_logits,
            "hg_norm_g": hg_norm_g, "ln1_g": ln1_g, "ln1_b": ln1_b, "w_gate": w_gate,
            "w_up": w_up, "w_down": w_down, "ln2_g": ln2_g, "ln2_b": ln2_b}

def reference(x, w_in, w_out, hg_lb_logits, hg_norm_g, ln1_g, ln1_b, w_gate, w_up, w_down, ln2_g, ln2_b):
    B, S, _ = x.shape
    f32 = jnp.float32
    lb_all = jnp.cumsum(jax.nn.softmax(hg_lb_logits.astype(f32), axis=0), axis=0)
    pts = _split_points()
    for l in range(DEPTH):
        proj = x @ w_in[l]
        dq, dk, dv, iq, ik, iw, hq, hf, hi, hg = jnp.split(proj, pts, axis=-1)
        a = _dsa_attention(dq.reshape(B, S, DSA_HEADS, DSA_HEAD_DIM),
                           dk.reshape(B, S, DSA_HEADS, DSA_HEAD_DIM),
                           dv.reshape(B, S, DSA_HEADS, DSA_HEAD_DIM),
                           iq.reshape(B, S, IDX_HEADS, IDX_DIM), ik, iw)
        lb = lb_all[l].reshape(HG_HEADS, HG_DK)
        o = _hgrn2(hq.reshape(B, S, HG_HEADS, HG_DK), hf.reshape(B, S, HG_HEADS, HG_DK),
                   hi.reshape(B, S, HG_HEADS, HG_DV), lb)
        o = o * lax.rsqrt(jnp.mean(jnp.square(o), axis=-1, keepdims=True) + RMS_EPS)
        r = o.reshape(B, S, HG_WIDTH) * hg_norm_g[l].astype(f32) * jax.nn.silu(hg.astype(f32))
        mix = jnp.concatenate([a, r.astype(x.dtype)], axis=-1) @ w_out[l]
        x = _layer_norm(ALPHA * x + mix, ln1_g[l], ln1_b[l])
        ff = (jax.nn.silu(x @ w_gate[l]) * (x @ w_up[l])) @ w_down[l]
        x = _layer_norm(ALPHA * x + ff, ln2_g[l], ln2_b[l])
    return x


_drawn_inputs = setup_inputs


def setup_inputs(seed=0):
    import zlib

    import numpy as np

    out = dict(_drawn_inputs(seed))
    spreads = {}
    factors = {'hg_lb_logits': 3.249,
     'hg_norm_g': 8.0,
     'ln1_g': 2.694,
     'ln1_b': 2.732,
     'ln2_g': 2.921,
     'ln2_b': 2.83}
    for name, (base, spread) in spreads.items():
        noise = np.random.default_rng([zlib.crc32(name.encode()), seed]).standard_normal(out[name].shape)
        drawn = base * np.exp(spread * noise) if base else spread * noise
        out[name] = __import__('jax').numpy.asarray(drawn.astype(out[name].dtype))
    for name, factor in factors.items():
        out[name] = (out[name] * factor).astype(out[name].dtype)
    return out
```

```python
from contextlib import ExitStack

import concourse.bass as bass
from concourse import mybir

F32 = mybir.dt.float32
F32R = mybir.dt.float32r
I32 = mybir.dt.int32
ALU = mybir.AluOpType
ACT = mybir.ActivationFunctionType

P = 128
SEQ, D = 512, 1024
TILES = SEQ // P
KT = D // P
HEADS, DH = 8, 64
TOPK = 128
HG = 4
CH = 64
NCH = SEQ // CH
FF = 2816
FT = FF // P
ALPHA = 2.0 ** 0.25
LN_EPS, RMS_EPS = 1e-5, 1e-6
IDX_SCALE = (64 ** -0.5) * (8 ** -0.5)
NEG = -3.0e38
TAKEN = -3.4e38
FAR = -1.0e30
LEVELS = [32, 16, 8, 4, 2, 1]

IN_SLABS = [("iq", 1536, 256), ("iq", 1792, 256), ("ik", 2048, 72),
            ("dk", 512, 256), ("dk", 768, 256), ("dq", 0, 256), ("dq", 256, 256),
            ("hf", 2632, 256), ("hf", 2888, 256), ("hq", 2120, 256), ("hq", 2376, 256),
            ("hi", 3144, 256), ("hi", 3400, 256), ("dv", 1024, 256), ("dv", 1280, 256),
            ("hg", 3656, 256), ("hg", 3912, 256)]
N_IN = len(IN_SLABS)
N_OUT = 4
W0 = N_IN
G0 = W0 + N_OUT
NPAIR = FT // 2
D0 = G0 + 2 * NPAIR
NDOWN = FT // 2

UNITS = []
for _n, (_kind, _c, _w) in enumerate(IN_SLABS):
    for _u in range(2 if _w == 256 else 1):
        UNITS.append((_n, _u, _kind))
NU = len(UNITS)
FIRST = {}
for _j, (_n, _u, _kind) in enumerate(UNITS):
    FIRST.setdefault(_kind, _j)
IDX_AFTER = 3
TOPK_FROM = 4
LEVEL_TILES = (3, 2, 1)


def build(nc, x, w_in, w_out, hg_lb_logits, hg_norm_g, ln1_g, ln1_b, w_gate, w_up, w_down,
          ln2_g, ln2_b, out):
    x_d = x.rearrange("a (i p) d -> p (a i) d", p=P)
    out_d = out.rearrange("a (i p) d -> p (a i) d", p=P)
    win_d = w_in.rearrange("a (k p) n -> p (a k) n", p=P)
    wout_d = w_out.rearrange("a (k p) n -> p (a k) n", p=P)
    gate_d = w_gate.rearrange("a (k p) n -> p (a k) n", p=P)
    up_d = w_up.rearrange("a (k p) n -> p (a k) n", p=P)
    down_d = w_down.rearrange("a (f p) n -> p (a f) n", p=P)

    with ExitStack() as ctx:
        def sem(name):
            return ctx.enter_context(nc.semaphore(name))

        base = [16512]

        def at(name, shape, dt, offset):
            return nc.alloc_sbuf_tensor_at(name, shape, dt, offset=offset)

        def keep(name, shape, dt=F32):
            size = 4
            for s in shape[1:]:
                size *= s
            t = at(name, shape, dt, base[0])
            base[0] += (size + 31) // 32 * 32
            return t

        arena = ctx.enter_context(nc.sbuf_tensor("arena", [P, 52000], F32))
        ident = keep("ident", [P, P])
        mean_w = keep("mean_w", [P, P])
        level_mask = keep("level_mask", [P, len(LEVELS), CH], I32)
        dist = keep("dist", [P, 512])
        keep_state = keep("keep_state", [P, 512])
        lb_l = keep("lb_l", [P, 2, HG])
        small = keep("small", [P, P])
        lb_e = keep("lb_e", [P, 2, HG])
        lb_m = keep("lb_m", [P, HG])
        lb = keep("lb", [P, HG])
        one_lb = keep("one_lb", [P, HG])
        norm_g = keep("norm_g", [P, HG])
        iw_n = keep("iw_n", [P, TILES, HEADS])
        top8 = keep("top8", [P, TILES, 8])
        nmax = keep("nmax", [P, HEADS * TILES])
        rsum = keep("rsum", [P, HEADS * TILES])
        rinv = keep("rinv", [P, HEADS * TILES])
        chunk_decay = keep("chunk_decay", [P, HG, NCH])
        stats = keep("stats", [P, 2 * TILES, 2, 6])
        moments = keep("moments", [P, 2 * TILES, 2])
        spread = keep("spread", [P, 2 * TILES])
        inv_spread = keep("inv_spread", [P, 2 * TILES])
        eps_ln = keep("eps_ln", [P, 1])
        eps_rms = keep("eps_rms", [P, 1])

        xT_hi = keep("xT_hi", [P, KT, SEQ], F32R)
        xT_lo = keep("xT_lo", [P, KT, SEQ], F32R)
        w_hi = keep("w_hi", [P, 2, 2048], F32R)
        w_lo = keep("w_lo", [P, 2, 2048], F32R)
        raw = keep("raw", [P, 2, 2048])
        zone = base[0]
        aT_hi = keep("aT_hi", [P, HG, SEQ], F32R)
        aT_lo = keep("aT_lo", [P, HG, SEQ], F32R)
        hqT = keep("hqT", [P, HG, SEQ])
        kkT = keep("kkT", [P, HG, SEQ])
        GT = keep("GT", [P, HG, SEQ])
        hvN = keep("hvN", [P, TILES, 512])
        hgT = keep("hgT", [P, HG, SEQ])
        shared = base[0]
        qT = keep("qT", [P, 4, SEQ])
        kT = keep("kT", [P, 4, SEQ])
        vN = keep("vN", [P, TILES, 512])
        SC0 = {1: 0, 2: 256, 3: 640}
        score = keep("score", [P, 1152])
        M0 = {0: 0, 1: 128, 2: 384, 3: 768}
        mask = keep("mask", [P, 1280])
        vtmp = keep("vtmp", [P, 2, SEQ])
        probs = keep("probs", [P, 2, SEQ])
        probsT = keep("probsT", [P, 2, TILES, SEQ])
        top = base[0]
        o = top - 16 * 1024
        iqT = at("iqT", [P, 4, SEQ], F32, o)
        ikT = at("ikT", [P, SEQ], F32, o + 8192)
        rel = at("rel", [P, 2, SEQ], F32, o + 10240)
        iwT = at("iwT", [P, SEQ], F32, o + 14336)
        x_in = at("x_in", [P, TILES, D], F32, shared)
        o = shared
        E0 = at("E0", [P, HG, SEQ], F32, o)
        E1 = at("E1", [P, HG, SEQ], F32, o + 8192)
        E = [E0, E1]
        AT = at("AT", [P, HG * TILES, P], F32, o + 16384)
        kdN = at("kdN", [P, HG * TILES, P], F32, o + 24576)
        state = at("state", [P, HG, NCH - 1, P], F32, o + 32768)
        oT = at("oT", [P, 2, SEQ], F32, o + 47104)
        sq = at("sq", [P, 2, SEQ], F32, o + 51200)
        rms = at("rms", [P, 2, SEQ], F32, o + 55296)
        assert o + 59392 <= 229344
        o = zone + 16384
        x1 = at("x1", [P, TILES, D], F32, shared)
        g1 = at("g1", [P, D], F32, o)
        b1 = at("b1", [P, D], F32, o + 4096)
        g2 = at("g2", [P, D], F32, o + 8192)
        b2 = at("b2", [P, D], F32, o + 12288)
        hT = at("hT", [P, FT, SEQ], F32, shared + 16384)
        assert shared + 16384 + FT * 2048 <= 229344
        silu_g = at("silu_g", [P, 2, 2, SEQ], F32, zone)
        h_hi = at("h_hi", [P, 2, 2, SEQ], F32R, zone + 32768)
        h_lo = at("h_lo", [P, 2, 2, SEQ], F32R, zone + 40960)
        assert zone + 49152 <= shared + 16384 and zone + 49152 <= shared + 1024 * 64
        y2 = at("y2", [P, TILES, D], F32, zone)
        assert top <= 229344, top
        assert zone + 49152 <= shared + 8192, (zone, shared)

        ps = ctx.enter_context(nc.psum_tensor("ps", [P, 8, 512], F32))

        x_loaded = [sem(f"x_loaded{i}") for i in range(TILES)]
        small_loaded, small_turned, small_out = sem("small_loaded"), sem("small_turned"), sem("small_out")
        raw_loaded = [sem(f"raw_loaded{i}") for i in range(2)]
        hi_done, lo_done = sem("hi_done"), sem("lo_done")
        out_used, down_used = sem("out_used"), sem("down_used")
        consts_ready = sem("consts_ready")
        xT_ps, xT_hi_done, xT_lo_done = sem("xT_ps"), sem("xT_hi_done"), sem("xT_lo_done")
        unit_done, unit_out = sem("unit_done"), sem("unit_out")
        vturn, vturn_out = sem("vturn"), sem("vturn_out")
        iw_turned, iw_ready = sem("iw_turned"), sem("iw_ready")
        idx_done, rel_done, acc_done = sem("idx_done"), sem("rel_done"), sem("acc_done")
        topk_step, mask_ready = sem("topk_step"), sem("mask_ready")
        qk_done, biased, masked = sem("qk_done"), sem("biased"), sem("masked")
        exp_done, rinv_done, normed = sem("exp_done"), sem("rinv_done"), sem("normed")
        pT_done, pT_out = sem("pT_done"), sem("pT_out")
        pv_done, a_hi_done, a_lo_done = sem("pv_done"), sem("a_hi_done"), sem("a_lo_done")
        lb_step, lb_exp = sem("lb_step"), sem("lb_exp")
        f_done, kk_done, ln_done, G_done = sem("f_done"), sem("kk_done"), sem("ln_done"), sem("G_done")
        hg_scaled = sem("hg_scaled")
        A_clear, A_step = sem("A_clear"), sem("A_step")
        lev_sub, lev_exp, lev_mul, lev_ps = sem("lev_sub"), sem("lev_exp"), sem("lev_mul"), sem("lev_ps")
        diag_ps = sem("diag_ps")
        kd_sub, kd_exp, kd_mul, kd_ps, kd_out = (sem(s) for s in ("kd_sub", "kd_exp", "kd_mul", "kd_ps", "kd_out"))
        qg_exp, qg_mul, cd_exp = sem("qg_exp"), sem("qg_mul"), sem("cd_exp")
        U_ps, state_step = sem("U_ps"), sem("state_step")
        o_ps, o_out, sq_done, ms_ps, rms_done, rms_inv = (sem(s) for s in ("o_ps", "o_out", "sq_done", "ms_ps", "rms_done", "rms_inv"))
        r_a, r_b, r_hi, r_lo = sem("r_a"), sem("r_b"), sem("r_hi"), sem("r_lo")
        x1_loaded, ln_par = [sem(f"x1_loaded{i}") for i in range(TILES)], sem("ln_par")
        res_done, ln_step, ln_root, ln_norm, ln_g, ln_b = (sem(s) for s in ("res_done", "ln_step", "ln_root", "ln_norm", "ln_g", "ln_b"))
        mix_done = sem("mix_done")
        x1T_ps, x1T_hi, x1T_lo = sem("x1T_ps"), sem("x1T_hi"), sem("x1T_lo")
        ff_ps, silu_done, h_done = sem("ff_ps"), sem("silu_done"), sem("h_done")
        hs_hi, hs_lo = sem("hs_hi"), sem("hs_lo")
        down_done = sem("down_done")
        stored = sem("stored")
        const_step = sem("const_step")

        block = ctx.enter_context(nc.Block())

        def hi_of(s, kt, c0, n, width):
            return w_hi[:, s, kt * width + c0:kt * width + c0 + n]

        def lo_of(s, kt, c0, n, width):
            return w_lo[:, s, kt * width + c0:kt * width + c0 + n]

        def wait_used(eng, n):
            if n < N_IN:
                eng.wait_ge(unit_done, sum(1 for m, _, _ in UNITS if m <= n))
            elif n < G0 - 1:
                eng.wait_ge(out_used, n - W0 + 1)
            elif n < G0:
                eng.wait_ge(mix_done, TILES)
            elif n < D0:
                eng.wait_ge(ff_ps, 2 * (n - G0) + 2)
            else:
                half, j = divmod(n - D0, NDOWN)
                if j < NDOWN - 1:
                    eng.wait_ge(down_used, half * (NDOWN - 1) + j + 1)
                else:
                    eng.wait_ge(down_done, TILES * (half + 1))

        def size_of(n):
            return KT * IN_SLABS[n][2] if n < N_IN else (2048 if n < D0 else 1024)

        @block.sync
        def _(sp):
            for i in range(TILES):
                sp.dma_start(x_in[:, i, :], x_d[:, i, :]).then_inc(x_loaded[i], 16)

            def free(n):
                if n >= 2:
                    sp.wait_ge(lo_done, n - 1)

            for n in range(N_IN):
                free(n)
                _, c, w = IN_SLABS[n]
                sp.dma_start(raw[:, n % 2, 0:KT * w].rearrange("p (k n) -> p k n", k=KT),
                             win_d[:, :, c:c + w]).then_inc(raw_loaded[n % 2], 16)
            for q in range(N_OUT):
                n = W0 + q
                free(n)
                k0, half = 4 * (q // 2), q % 2
                sp.dma_start(raw[:, n % 2, :].rearrange("p (k n) -> p k n", k=4),
                             wout_d[:, k0:k0 + 4, half * 512:half * 512 + 512]).then_inc(raw_loaded[n % 2], 16)
            for j in range(NPAIR):
                for v, w_d in enumerate((gate_d, up_d)):
                    n = G0 + 2 * j + v
                    free(n)
                    sp.dma_start(raw[:, n % 2, :].rearrange("p (k n) -> p k n", k=KT),
                                 w_d[:, :, 256 * j:256 * j + 256]).then_inc(raw_loaded[n % 2], 16)
            for half in range(2):
                for j in range(NDOWN):
                    n = D0 + NDOWN * half + j
                    free(n)
                    sp.dma_start(raw[:, n % 2, 0:1024].rearrange("p (k n) -> p k n", k=2),
                                 down_d[:, 2 * j:2 * j + 2, half * 512:half * 512 + 512]
                                 ).then_inc(raw_loaded[n % 2], 16)
            for i in range(TILES):
                sp.wait_ge(ln_b, TILES + i + 1)
                sp.dma_start(out_d[:, i, :], y2[:, i, :]).then_inc(stored, 16)
            sp.wait_ge(stored, 16 * TILES)

        @block.tensor
        def _(pe):
            mm, turn = nc.tensor.matmul, nc.tensor.transpose

            pe.wait_ge(consts_ready, 1)
            pe.wait_ge(small_loaded, 32)
            turn(ps[:, 3, 0:12], small[0:12, :], ident[0:12, 0:12]).then_inc(small_turned, 1)
            for kt in range(KT):
                if kt >= 4:
                    pe.wait_ge(xT_lo_done, kt - 3)
                for i in range(TILES):
                    if kt == 0:
                        pe.wait_ge(x_loaded[i], 16)
                    last = turn(ps[:, 4 + kt % 4, i * P:(i + 1) * P], x_in[:, i, kt * P:(kt + 1) * P], ident[:])
                last.then_inc(xT_ps, 1)

            def unit(j):
                n, u, kind = UNITS[j]
                w = IN_SLABS[n][2]
                m = 128 if w == 256 else w
                s = n % 2
                if u == 0:
                    pe.wait_ge(lo_done, n + 1)
                if j >= 2:
                    pe.wait_ge(unit_out, j - 1)
                for kt in range(KT):
                    if j == 0:
                        pe.wait_ge(xT_lo_done, kt + 1)
                    hi, lo = hi_of(s, kt, u * P, m, w), lo_of(s, kt, u * P, m, w)
                    o = ps[0:m, j % 2, :]
                    mm(o, hi, xT_hi[:, kt, :], start=(kt == 0), stop=False)
                    mm(o, hi, xT_lo[:, kt, :], start=False, stop=False)
                    last = mm(o, lo, xT_hi[:, kt, :], start=False, stop=(kt == KT - 1))
                last.then_inc(unit_done, 1)

            def turn_v(j):
                t = (j - FIRST["hi"])
                pe.wait_ge(unit_out, j + 1)
                if t >= 2:
                    pe.wait_ge(vturn_out, t - 1)
                for i in range(TILES):
                    last = turn(ps[:, 4 + t % 2, i * P:(i + 1) * P], vtmp[:, t % 2, i * P:(i + 1) * P], ident[:])
                last.then_inc(vturn, 1)

            def index():
                pe.wait_ge(unit_out, FIRST["ik"] + 1)
                pe.wait_ge(xT_lo_done, KT)
                for i in range(TILES):
                    last = turn(ps[:, 4, i * 8:i * 8 + 8], iwT[0:8, i * P:(i + 1) * P], ident[0:8, 0:8])
                last.then_inc(iw_turned, 1)
                j = 0
                for h in range(HEADS):
                    a = 64 * (h % 2)
                    for i in LEVEL_TILES:
                        if j >= 2:
                            pe.wait_ge(rel_done, j - 1)
                        mm(ps[:, 2 + j % 2, 0:P * (i + 1)], iqT[a:a + 64, h // 2, i * P:(i + 1) * P],
                           ikT[a:a + 64, 0:P * (i + 1)], start=True, stop=True).then_inc(idx_done, 1)
                        j += 1

            vfirst, vlast = FIRST["hi"], FIRST["hg"] - 1
            for j in range(NU):
                unit(j)
                if vfirst <= j - 1 <= vlast:
                    turn_v(j - 1)
                if UNITS[j][0] == IDX_AFTER and UNITS[j][1] == 1:
                    index()

            def qk(a):
                h, i = a // 4, a % 4
                b = 64 * (h % 2)
                if a >= 2:
                    pe.wait_ge(biased, a - 1)
                mm(ps[:, 2 + a % 2, 0:P * (i + 1)], qT[b:b + 64, h // 2, i * P:(i + 1) * P],
                   kT[b:b + 64, h // 2, 0:P * (i + 1)], start=True, stop=True).then_inc(qk_done, 1)

            def turn_p(a):
                i = a % 4
                pe.wait_ge(normed, a + 1)
                if a >= 2:
                    pe.wait_ge(pT_out, a - 1)
                for j in range(i + 1):
                    last = turn(ps[:, 4 + a % 2, j * P:(j + 1) * P], probs[:, a % 2, j * P:(j + 1) * P], ident[:])
                last.then_inc(pT_done, 1)

            def pv(h):
                pe.wait_ge(pT_out, 4 * h + 4)
                g, b = h // 2, 64 * (h % 2)
                if h >= 4:
                    pe.wait_ge(a_lo_done, g - 1)
                for j in range(TILES):
                    last = mm(ps[b:b + 64, 6 + g % 2, j * P:SEQ], vN[:, j, h * DH:(h + 1) * DH],
                              probsT[:, h % 2, j, j * P:SEQ], start=(j == 0), stop=(j == TILES - 1))
                last.then_inc(pv_done, 1)

            pe.wait_ge(unit_out, NU)
            pe.wait_ge(vturn_out, 8)
            qk(0)
            for a in range(HEADS * TILES):
                if a + 1 < HEADS * TILES:
                    qk(a + 1)
                turn_p(a)
                if a >= 4 and a % 4 == 1:
                    pv(a // 4 - 1)
            pv(HEADS - 1)

            pe.wait_ge(a_lo_done, 4)
            pe.wait_ge(kk_done, HG)
            pe.wait_ge(unit_out, NU)
            for p in range(HG * TILES):
                last = mm(ps[:, 4 + p // 4, (p % 4) * P:(p % 4 + 1) * P], kkT[:, p // 4, (p % 4) * P:(p % 4 + 1) * P],
                          hqT[:, p // 4, (p % 4) * P:(p % 4 + 1) * P], start=(p % 4 == 0), stop=(p % 4 == 3),
                          skip_group_check=True)
                if p % 4 == 3:
                    last.then_inc(diag_ps, 1)
            for l, m in enumerate(LEVELS):
                pe.wait_ge(lev_mul, 2 * (l + 1))
                if l >= 2:
                    pe.wait_ge(A_step, 4 + 2 * (l - 1))
                for p in range(HG * TILES):
                    X = E[l % 2][:, p // 4, (p % 4) * P:(p % 4 + 1) * P]
                    second = X.rearrange("p (b t) -> p b t", t=2 * m)[:, :, m:2 * m]
                    last = mm(ps[:, 2 * (l % 2) + p // 8, (p % 8) * CH:(p % 8 + 1) * CH].rearrange(
                        "p (b t) -> p b t", t=m), X, second, start=(p % 8 == 0), stop=(p % 8 == 7), skip_group_check=True)
                    if p % 8 == 7:
                        last.then_inc(lev_ps, 1)
            pe.wait_ge(kd_mul, 1)
            pe.wait_ge(A_step, 4)
            for p in range(HG * TILES):
                last = turn(ps[:, 4 + p // 4, (p % 4) * P:(p % 4 + 1) * P], E0[:, p // 4, (p % 4) * P:(p % 4 + 1) * P], ident[:])
                if p % 4 == 3:
                    last.then_inc(kd_ps, 1)
            pe.wait_ge(A_step, 4 + 2 * len(LEVELS))
            for h in range(HG):
                pe.wait_ge(kd_out, h + 1)
                if h >= 2:
                    pe.wait_ge(state_step, (h - 1) * (NCH - 1))
                for c in range(NCH - 1):
                    b = CH * (c % 2)
                    f = (c // 2) * P
                    last = mm(ps[:, 2 * (h % 2) + c % 2, f:f + P], kdN[b:b + CH, 4 * h + c // 2, :],
                              hvN[b:b + CH, c // 2, h * P:(h + 1) * P], start=(c < 2), stop=(c >= NCH - 3),
                              skip_group_check=True)
                last.then_inc(U_ps, 1)
            pe.wait_ge(qg_mul, 1)
            pe.wait_ge(kd_out, HG)
            for h in range(HG):
                bank = 4 + h % 2
                pe.wait_ge(state_step, (h + 1) * (NCH - 1))
                if h >= 2:
                    pe.wait_ge(sq_done, h - 1)
                    pe.wait_ge(o_out, h - 1)
                for p in range(TILES):
                    mm(ps[:, bank, p * P:(p + 1) * P], hvN[:, p, h * P:(h + 1) * P], AT[:, 4 * h + p, :],
                       start=(p == 0), stop=False, skip_group_check=True)
                for c in range(1, NCH):
                    last = mm(ps[:, bank, c * CH:(c + 1) * CH], state[:, h, c - 1, :], E1[:, h, c * CH:(c + 1) * CH],
                              start=False, stop=(c == NCH - 1), skip_group_check=True)
                last.then_inc(o_ps, 1)
                pe.wait_ge(sq_done, h + 1)
                if h >= 2:
                    pe.wait_ge(rms_done, h - 1)
                mm(ps[:, 6 + h % 2, :], mean_w[:], sq[:, h % 2, :], start=True, stop=True).then_inc(ms_ps, 1)

            for q in range(N_OUT):
                n = W0 + q
                pe.wait_ge(lo_done, n + 1)
                if q == 0:
                    pe.wait_ge(rms_done, HG)
                if q == 2:
                    pe.wait_ge(r_lo, HG)
                for kk in range(4):
                    for i in range(TILES):
                        c_hi, c_lo = (aT_hi, aT_lo) if q < 2 else (xT_hi, xT_lo)
                        o = ps[:, 4 * (q % 2) + i, :]
                        hi, lo = w_hi[:, n % 2, kk * 512:(kk + 1) * 512], w_lo[:, n % 2, kk * 512:(kk + 1) * 512]
                        a_hi, a_lo = c_hi[:, kk, i * P:(i + 1) * P], c_lo[:, kk, i * P:(i + 1) * P]
                        first, end = q < 2 and kk == 0, q >= 2 and kk == 3
                        mm(o, a_hi, hi, start=first, stop=False)
                        mm(o, a_hi, lo, start=False, stop=False)
                        last = mm(o, a_lo, hi, start=False, stop=end)
                        if q == 3 and kk == 3:
                            last.then_inc(mix_done, 1)
                if q < 3:
                    last.then_inc(out_used, 1)

            for i in range(TILES):
                pe.wait_ge(ln_b, i + 1)
                for kt in range(KT):
                    last = turn(ps[:, (0 if kt < 4 else 4) + i, (kt % 4) * P:(kt % 4 + 1) * P],
                                x1[:, i, kt * P:(kt + 1) * P], ident[:])
                last.then_inc(x1T_ps, 1)

            pe.wait_ge(x1T_lo, 2 * TILES)
            for j in range(NPAIR):
                for v in range(2):
                    n = G0 + 2 * j + v
                    pe.wait_ge(lo_done, n + 1)
                    if j >= 2:
                        pe.wait_ge(h_done, 2 * (j - 1))
                    for u in range(2):
                        o = ps[:, 4 * (j % 2) + 2 * v + u, :]
                        for kt in range(KT):
                            hi, lo = hi_of(n % 2, kt, u * P, P, 256), lo_of(n % 2, kt, u * P, P, 256)
                            mm(o, hi, xT_hi[:, kt, :], start=(kt == 0), stop=False)
                            mm(o, hi, xT_lo[:, kt, :], start=False, stop=False)
                            last = mm(o, lo, xT_hi[:, kt, :], start=False, stop=(kt == KT - 1))
                        last.then_inc(ff_ps, 1)

            pe.wait_ge(h_done, 2 * NPAIR)
            for half in range(2):
                for j in range(NDOWN):
                    q = NDOWN * half + j
                    n = D0 + q
                    pe.wait_ge(lo_done, n + 1)
                    pe.wait_ge(hs_lo, q + 1)
                    for kk in range(2):
                        for i in range(TILES):
                            o = ps[:, 4 * half + i, :]
                            hi, lo = w_hi[:, n % 2, kk * 512:(kk + 1) * 512], w_lo[:, n % 2, kk * 512:(kk + 1) * 512]
                            a_hi, a_lo = h_hi[:, q % 2, kk, i * P:(i + 1) * P], h_lo[:, q % 2, kk, i * P:(i + 1) * P]
                            mm(o, a_hi, hi, start=(j == 0 and kk == 0), stop=False)
                            mm(o, a_hi, lo, start=False, stop=False)
                            last = mm(o, a_lo, hi, start=False, stop=(j == NDOWN - 1 and kk == 1))
                            if j == NDOWN - 1 and kk == 1:
                                last.then_inc(down_done, 1)
                    if j < NDOWN - 1:
                        last.then_inc(down_used, 1)

        @block.scalar
        def _(act):
            def cp(o, i, scale=1.0):
                return nc.scalar.activation(o, i, ACT.Copy, scale=scale)

            def split_hi(n):
                act.wait_ge(raw_loaded[n % 2], 16 * (n // 2 + 1))
                if n >= 2:
                    wait_used(act, n - 2)
                size = size_of(n)
                cp(w_hi[:, n % 2, 0:size], raw[:, n % 2, 0:size]).then_inc(hi_done, 1)

            act.dma_start(small[0:8, :], hg_lb_logits.rearrange("l (h k) -> (l h) k", k=P)).then_inc(small_loaded, 16)
            act.dma_start(small[8:12, :], hg_norm_g.rearrange("a (h v) -> (a h) v", v=P)).then_inc(small_loaded, 16)
            act.wait_ge(lb_step, 2)
            nc.scalar.activation(lb_e[:], lb_e[:], ACT.Exp).then_inc(lb_exp, 1)
            for kt in range(KT):
                act.wait_ge(xT_ps, kt + 1)
                cp(xT_hi[:, kt, :], ps[:, 4 + kt % 4, :]).then_inc(xT_hi_done, 1)
                if kt == 3:
                    split_hi(0)
                if kt == 5:
                    split_hi(1)

            def out_of(j):
                n, u, kind = UNITS[j]
                act.wait_ge(unit_done, j + 1)
                g = j - FIRST[kind]
                src = ps[:, j % 2, :]
                if kind == "iq":
                    cp(iqT[:, g, :], src).then_inc(unit_out, 1)
                elif kind == "ik":
                    cp(ikT[0:64, :], ps[0:64, j % 2, :])
                    cp(ikT[64:128, :], ps[0:64, j % 2, :])
                    cp(iwT[0:8, :], ps[64:72, j % 2, :]).then_inc(unit_out, 1)
                elif kind == "dk":
                    cp(kT[:, g, :], src).then_inc(unit_out, 1)
                elif kind == "dq":
                    cp(qT[:, g, :], src, DH ** -0.5).then_inc(unit_out, 1)
                elif kind == "hf":
                    nc.scalar.activation(kkT[:, g, :], src, ACT.Sigmoid).then_inc(unit_out, 1)
                elif kind == "hq":
                    cp(hqT[:, g, :], src).then_inc(unit_out, 1)
                elif kind in ("hi", "dv"):
                    t = j - FIRST["hi"]
                    if t >= 2:
                        act.wait_ge(vturn, t - 1)
                    cp(vtmp[:, t % 2, :], src).then_inc(unit_out, 1)
                else:
                    nc.scalar.activation(hgT[:, g, :], src, ACT.Silu).then_inc(unit_out, 1)

            def turned_v(j):
                t = j - FIRST["hi"]
                act.wait_ge(vturn, t + 1)
                dst = hvN if t < 4 else vN
                g = t % 4
                cp(dst[:, :, g * P:(g + 1) * P], ps[:, 4 + t % 2, :].rearrange("p (i f) -> p i f", i=TILES)
                   ).then_inc(vturn_out, 1)

            def relus():
                act.wait_ge(iw_turned, 1)
                cp(iw_n[:].rearrange("p i h -> p (i h)"), ps[:, 4, 0:32], IDX_SCALE).then_inc(iw_ready, 1)
                j = 0
                for h in range(HEADS):
                    for i in LEVEL_TILES:
                        act.wait_ge(idx_done, j + 1)
                        if j >= 2:
                            act.wait_ge(acc_done, j - 1)
                        nc.scalar.activation(rel[:, j % 2, 0:P * (i + 1)], ps[:, 2 + j % 2, 0:P * (i + 1)],
                                             ACT.Relu).then_inc(rel_done, 1)
                        j += 1

            for j in range(NU):
                n, u, kind = UNITS[j]
                out_of(j)
                if FIRST["hi"] <= j - 1 < FIRST["hg"]:
                    turned_v(j - 1)
                if u == 1 or kind == "ik":
                    if n + 2 < G0:
                        split_hi(n + 2)
                if kind == "hq" and u == 1 and n == 10:
                    for g in range(HG):
                        act.wait_ge(kk_done, g + 1)
                        nc.scalar.activation(GT[:, g, :], GT[:, g, :], ACT.Ln).then_inc(ln_done, 1)
                if n == IDX_AFTER and u == 1:
                    relus()

            def exps(a):
                i = a % 4
                act.wait_ge(masked, a + 1)
                nc.scalar.activation(probs[:, a % 2, 0:P * (i + 1)], probs[:, a % 2, 0:P * (i + 1)], ACT.Exp,
                                     bias=nmax[:, a:a + 1], scale=-1.0, accum_out=rsum[:, a:a + 1]).then_inc(exp_done, 1)

            def turned_p(a):
                h, i = a // 4, a % 4
                act.wait_ge(pT_done, a + 1)
                if h >= 2 and i == 0:
                    act.wait_ge(pv_done, h - 1)
                cp(probsT[:, h % 2, 0:i + 1, i * P:(i + 1) * P],
                   ps[:, 4 + a % 2, 0:P * (i + 1)].rearrange("p (j q) -> p j q", q=P)).then_inc(pT_out, 1)

            def a_out(g):
                act.wait_ge(pv_done, 2 * g + 2)
                cp(aT_hi[:, g, :], ps[:, 6 + g % 2, :]).then_inc(a_hi_done, 1)

            act.wait_ge(topk_step, 96)
            exps(0)
            for a in range(HEADS * TILES):
                if a + 1 < HEADS * TILES:
                    exps(a + 1)
                turned_p(a)
                if a >= 8 and a % 8 == 3:
                    a_out(a // 8 - 1)
            a_out(3)

            for l in range(len(LEVELS)):
                act.wait_ge(lev_sub, 2 * (l + 1))
                nc.scalar.activation(E[l % 2][:], E[l % 2][:], ACT.Exp).then_inc(lev_exp, 1)
            nc.scalar.activation(chunk_decay[:], GT[:].rearrange("p h (c t) -> p h c t", t=CH)[:, :, :, CH - 1],
                                 ACT.Exp).then_inc(cd_exp, 1)
            act.wait_ge(kd_sub, 1)
            nc.scalar.activation(E0[:], E0[:], ACT.Exp).then_inc(kd_exp, 1)
            act.wait_ge(lev_ps, 2 * len(LEVELS))
            nc.scalar.activation(E1[:], GT[:], ACT.Exp).then_inc(qg_exp, 1)
            for h in range(HG):
                act.wait_ge(kd_ps, h + 1)
                cp(kdN[:, 4 * h:4 * h + 4, :], ps[:, 4 + h, :].rearrange("p (a k) -> p a k", k=P)).then_inc(kd_out, 1)
            for h in range(HG):
                act.wait_ge(o_ps, h + 1)
                if h >= 2:
                    act.wait_ge(r_a, h - 1)
                    act.wait_ge(ms_ps, h - 1)
                cp(oT[:, h % 2, :], ps[:, 4 + h % 2, :]).then_inc(o_out, 1)
                nc.scalar.activation(sq[:, h % 2, :], ps[:, 4 + h % 2, :], ACT.Square).then_inc(sq_done, 1)
                act.wait_ge(ms_ps, h + 1)
                if h >= 2:
                    act.wait_ge(r_a, h - 1)
                nc.scalar.activation(rms[:, h % 2, :], ps[:, 6 + h % 2, :], ACT.Sqrt, bias=eps_rms[:, 0:1]).then_inc(rms_done, 1)
                act.wait_ge(r_b, h + 1)
                cp(xT_hi[:, h, :], oT[:, h % 2, :]).then_inc(r_hi, 1)

            act.wait_ge(r_lo, HG)
            for i in range(TILES):
                act.dma_start(x1[:, i, :], x_d[:, i, :]).then_inc(x1_loaded[i], 16)
            for t, v in ((g1, ln1_g), (b1, ln1_b), (g2, ln2_g), (b2, ln2_b)):
                act.dma_start(t[:], v.partition_broadcast(P).rearrange("p a d -> p (a d)")).then_inc(ln_par, 16)
            split_hi(W0 + 2)
            split_hi(W0 + 3)

            def root(s, i):
                act.wait_ge(ln_step, 2 * (s * TILES + i) + 2)
                k = s * TILES + i
                nc.scalar.activation(spread[:, k:k + 1], moments[:, k, 1:2], ACT.Sqrt, bias=eps_ln[:, 0:1]
                                     ).then_inc(ln_root, 1)

            split_hi(G0)
            for i in range(TILES):
                root(0, i)
            split_hi(G0 + 1)
            for i in range(TILES):
                act.wait_ge(x1T_ps, i + 1)
                for b in range(2):
                    cp(xT_hi[:, 4 * b:4 * b + 4, i * P:(i + 1) * P],
                       ps[:, 4 * b + i, :].rearrange("p (k t) -> p k t", k=4)).then_inc(x1T_hi, 1)

            for j in range(NPAIR):
                for u in range(2):
                    act.wait_ge(ff_ps, 4 * j + u + 1)
                    if j >= 2:
                        act.wait_ge(h_done, 2 * (j - 2) + u + 1)
                    nc.scalar.activation(silu_g[:, j % 2, u, :], ps[:, 4 * (j % 2) + u, :], ACT.Silu).then_inc(silu_done, 1)
                split_hi(G0 + 2 * j + 2)
                split_hi(G0 + 2 * j + 3)

            for q in range(2 * NDOWN):
                j = q % NDOWN
                if q == 0:
                    act.wait_ge(h_done, 2 * NPAIR)
                if q >= 2:
                    wait_used(act, D0 + q - 2)
                cp(h_hi[:, q % 2, :, :], hT[:, 2 * j:2 * j + 2, :]).then_inc(hs_hi, 1)
                if q + 2 < 2 * NDOWN:
                    split_hi(D0 + q + 2)
            for i in range(TILES):
                root(1, i)

        @block.vector
        def _(dve):
            def split_lo(n):
                dve.wait_ge(hi_done, n + 1)
                size = size_of(n)
                nc.vector.tensor_tensor(w_lo[:, n % 2, 0:size], raw[:, n % 2, 0:size],
                                        w_hi[:, n % 2, 0:size].bitcast(F32), ALU.subtract).then_inc(lo_done, 1)

            nc.vector.memset(eps_ln[:], LN_EPS)
            nc.vector.memset(eps_rms[:], RMS_EPS)
            dve.wait_ge(small_turned, 1)
            nc.vector.tensor_copy(lb_l[:].rearrange("p l h -> p (l h)"), ps[:, 3, 0:8]).then_inc(small_out, 1)
            nc.vector.tensor_copy(norm_g[:], ps[:, 3, 8:12]).then_inc(small_out, 1)
            dve.wait_ge(small_out, 2)
            nc.vector.tensor_tensor(lb_m[:], lb_l[:, 0, :], lb_l[:, 1, :], ALU.max).then_inc(lb_step, 1)
            dve.wait_ge(lb_step, 1)
            nc.vector.tensor_tensor(lb_e[:], lb_l[:], lb_m[:].unsqueeze(1).broadcast_to([P, 2, HG]),
                                    ALU.subtract).then_inc(lb_step, 1)
            dve.wait_ge(lb_exp, 1)
            nc.vector.tensor_tensor(lb_m[:], lb_e[:, 0, :], lb_e[:, 1, :], ALU.add).then_inc(lb_step, 1)
            dve.wait_ge(lb_step, 3)
            nc.vector.reciprocal(lb_m[:], lb_m[:]).then_inc(lb_step, 1)
            dve.wait_ge(lb_step, 4)
            nc.vector.tensor_tensor(lb[:], lb_e[:, 0, :], lb_m[:], ALU.mult).then_inc(lb_step, 1)
            dve.wait_ge(lb_step, 5)
            nc.vector.tensor_scalar(one_lb[:], lb[:], -1.0, 1.0, ALU.mult, ALU.add).then_inc(lb_step, 1)

            for kt in range(KT):
                dve.wait_ge(xT_hi_done, kt + 1)
                nc.vector.tensor_tensor(xT_lo[:, kt, :], ps[:, 4 + kt % 4, :], xT_hi[:, kt, :].bitcast(F32),
                                        ALU.subtract).then_inc(xT_lo_done, 1)
                if kt == 4:
                    split_lo(0)
                if kt == 6:
                    split_lo(1)

            nc.vector.memset(mask[:, 0:P], 0.0).then_inc(mask_ready, 1)
            dve.wait_ge(mask_ready, 1)
            nc.vector.memset(mask[0:64, 64:P], FAR).then_inc(mask_ready, 1)

            def sc(i):
                return score[:, SC0[i]:SC0[i] + P * (i + 1)]

            def scores():
                dve.wait_ge(iw_ready, 1)
                j = 0
                for h in range(HEADS):
                    for i in LEVEL_TILES:
                        dve.wait_ge(rel_done, j + 1)
                        r = rel[:, j % 2, 0:P * (i + 1)]
                        if h == 0:
                            ins = nc.vector.tensor_scalar(sc(i), r, iw_n[:, i, h:h + 1], None, ALU.mult)
                        else:
                            dve.wait_ge(acc_done, j - 2)
                            ins = nc.vector.scalar_tensor_tensor(out=sc(i), in0=r, scalar=iw_n[:, i, h:h + 1],
                                                                 in1=sc(i), op0=ALU.mult, op1=ALU.add)
                        ins.then_inc(acc_done, 1)
                        j += 1
                dve.wait_ge(acc_done, 24)
                for i in LEVEL_TILES:
                    nc.vector.memset(score[0:64, SC0[i] + P * i + 64:SC0[i] + P * (i + 1)], NEG).then_inc(acc_done, 1)
                dve.wait_ge(acc_done, 27)

            steps = [(r, op, i) for r in range(TOPK // 8) for op in ("max", "take") for i in LEVEL_TILES]

            def select_keys(a, b):
                for k in range(a, min(b, len(steps))):
                    r, op, i = steps[k]
                    if k >= 3:
                        dve.wait_ge(topk_step, k - 2)
                    if op == "max":
                        nc.vector.max(out=top8[:, i, :], in_=sc(i)).then_inc(topk_step, 1)
                    else:
                        nc.vector.match_replace(out=sc(i), in_to_replace=top8[:, i, :], in_values=sc(i),
                                                imm_value=TAKEN).then_inc(topk_step, 1)

            done = 0
            for n in range(N_IN):
                if n >= 7:
                    g = n - 7
                    if g in (4, 5, 6, 7):
                        g -= 4
                        dve.wait_ge(ln_done, g + 1)
                        nc.vector.tensor_tensor_scan(out=GT[:, g, :], data0=keep_state[:], data1=GT[:, g, :],
                                                     initial=0.0, op0=ALU.mult, op1=ALU.add).then_inc(G_done, 1)
                if n + 2 < G0:
                    split_lo(n + 2)
                if n == IDX_AFTER:
                    scores()
                if n >= TOPK_FROM:
                    select_keys(done, done + 9)
                    done += 9
            select_keys(done, len(steps))
            dve.wait_ge(topk_step, len(steps))
            for i in LEVEL_TILES:
                nc.vector.tensor_scalar(mask[:, M0[i]:M0[i] + P * (i + 1)], sc(i), TAKEN, FAR, ALU.not_equal,
                                        ALU.mult).then_inc(mask_ready, 1)
            dve.wait_ge(mask_ready, 5)

            def bias(a):
                h, i = a // 4, a % 4
                n = P * (i + 1)
                pr = probs[:, a % 2, 0:n]
                dve.wait_ge(qk_done, a + 1)
                if a >= 2:
                    dve.wait_ge(pT_done, a - 1)
                nc.vector.scalar_tensor_tensor(out=pr, in0=dist[:, 384 - P * i:384 - P * i + n],
                                               scalar=-(2.0 ** -(h + 1)), in1=ps[:, 2 + a % 2, 0:n],
                                               op0=ALU.mult, op1=ALU.add).then_inc(biased, 1)
                dve.wait_ge(biased, a + 1)
                nc.vector.tensor_tensor_reduce(out=pr, in0=pr, in1=mask[:, M0[i]:M0[i] + n], scale=-1.0, scalar=3.0e38,
                                               op0=ALU.add, op1=ALU.min, accum_out=nmax[:, a:a + 1]).then_inc(masked, 1)

            def inverse(a):
                dve.wait_ge(exp_done, a + 1)
                nc.vector.reciprocal(rinv[:, a:a + 1], rsum[:, a:a + 1]).then_inc(rinv_done, 1)

            def a_low(g):
                dve.wait_ge(a_hi_done, g + 1)
                nc.vector.tensor_tensor(aT_lo[:, g, :], ps[:, 6 + g % 2, :], aT_hi[:, g, :].bitcast(F32),
                                        ALU.subtract).then_inc(a_lo_done, 1)

            bias(0)
            for a in range(HEADS * TILES):
                if a + 1 < HEADS * TILES:
                    bias(a + 1)
                inverse(a)
                if a >= 8 and a % 8 == 4:
                    a_low(a // 8 - 1)
            a_low(3)

            dve.wait_ge(A_clear, 1)
            for h in range(HG):
                dve.wait_ge(diag_ps, h + 1)
                nc.vector.copy_predicated(out=AT[:, 4 * h:4 * h + 4, :],
                                          mask=ident[:].bitcast(I32).unsqueeze(1).broadcast_to([P, 4, P]),
                                          data=ps[:, 4 + h, :].rearrange("p (a t) -> p a t", t=P)).then_inc(A_step, 1)
            for l, m in enumerate(LEVELS):
                for b in range(2):
                    dve.wait_ge(lev_ps, 2 * l + b + 1)
                    dve.wait_ge(A_step, 4 if l == 0 else 3 + 2 * l + b)
                    dst = AT[:, 8 * b:8 * b + 8, :].rearrange("p a (b t) -> p a b t", t=2 * m)[:, :, :, m:2 * m]
                    msk = level_mask[:, l, :].rearrange("p (b t) -> p b t", t=m).unsqueeze(1).broadcast_to([P, 8, CH // m, m])
                    src = ps[:, 2 * (l % 2) + b, :].rearrange("p (a b t) -> p a b t", a=8, t=m)
                    nc.vector.copy_predicated(out=dst, mask=msk, data=src).then_inc(A_step, 1)
            dve.wait_ge(cd_exp, 1)
            for h in range(HG):
                dve.wait_ge(U_ps, h + 1)
                for c in range(NCH - 1):
                    U = ps[:, 2 * (h % 2) + c % 2, (c // 2) * P:(c // 2 + 1) * P]
                    if c == 0:
                        ins = nc.vector.tensor_copy(state[:, h, c, :], U)
                    else:
                        dve.wait_ge(state_step, h * (NCH - 1) + c)
                        ins = nc.vector.scalar_tensor_tensor(out=state[:, h, c, :], in0=state[:, h, c - 1, :],
                                                             scalar=chunk_decay[:, h, c:c + 1], in1=U,
                                                             op0=ALU.mult, op1=ALU.add)
                    ins.then_inc(state_step, 1)
            for h in range(HG):
                r, o_ = rms[:, h % 2, :], oT[:, h % 2, :]
                dve.wait_ge(rms_done, h + 1)
                nc.vector.reciprocal(r, r).then_inc(rms_inv, 1)
                dve.wait_ge(rms_inv, h + 1)
                dve.wait_ge(o_out, h + 1)
                nc.vector.tensor_tensor(o_, o_, r, ALU.mult).then_inc(r_a, 1)
                dve.wait_ge(r_a, h + 1)
                dve.wait_ge(hg_scaled, h + 1)
                nc.vector.tensor_tensor(o_, o_, hgT[:, h, :], ALU.mult).then_inc(r_b, 1)
                dve.wait_ge(r_hi, h + 1)
                nc.vector.tensor_tensor(xT_lo[:, h, :], o_, xT_hi[:, h, :].bitcast(F32), ALU.subtract).then_inc(r_lo, 1)

            def residual(s, i, half):
                src, dst = (x1, x1) if s == 0 else (x1, y2)
                c = slice(half * 512, half * 512 + 512)
                k = s * TILES + i
                nc.vector.scalar_tensor_tensor(out=dst[:, i, c], in0=src[:, i, c], scalar=ALPHA,
                                               in1=ps[:, 4 * half + i, :], op0=ALU.mult, op1=ALU.add).then_inc(res_done, 1)

            def half_stats(s, i, half, count):
                c = slice(half * 512, half * 512 + 512)
                t = x1 if s == 0 else y2
                dve.wait_ge(res_done, count)
                return nc.vector.bn_stats(out=stats[:, s * TILES + i, half, :], in_=t[:, i, c])

            def aggregate(s, i):
                k = s * TILES + i
                dve.wait_ge(ln_step, 2 * k + 1)
                nc.vector.bn_aggr(out=moments[:, k, :], in_=stats[:, k, :, :]).then_inc(ln_step, 1)

            def normalise(s, i):
                k = s * TILES + i
                t = x1 if s == 0 else y2
                dve.wait_ge(ln_root, k + 1)
                nc.vector.reciprocal(inv_spread[:, k:k + 1], spread[:, k:k + 1]).then_inc(rms_inv, 1)
                dve.wait_ge(rms_inv, HG + k + 1)
                nc.vector.tensor_scalar(t[:, i, :], t[:, i, :], moments[:, k, 0:1], inv_spread[:, k:k + 1],
                                        ALU.subtract, ALU.mult).then_inc(ln_norm, 1)

            split_lo(W0 + 2)
            split_lo(W0 + 3)
            split_lo(G0)
            for i in range(TILES):
                dve.wait_ge(mix_done, i + 1)
                dve.wait_ge(x1_loaded[i], 16)
                for half in range(2):
                    residual(0, i, half)
                for half in range(2):
                    ins = half_stats(0, i, half, 2 * i + half + 1)
                ins.then_inc(ln_step, 1)
                aggregate(0, i)
                if i >= 1:
                    normalise(0, i - 1)
            normalise(0, TILES - 1)
            split_lo(G0 + 1)
            for i in range(TILES):
                for b in range(2):
                    dve.wait_ge(x1T_hi, 2 * i + b + 1)
                    nc.vector.tensor_tensor(xT_lo[:, 4 * b:4 * b + 4, i * P:(i + 1) * P],
                                            ps[:, 4 * b + i, :].rearrange("p (k t) -> p k t", k=4),
                                            xT_hi[:, 4 * b:4 * b + 4, i * P:(i + 1) * P].bitcast(F32),
                                            ALU.subtract).then_inc(x1T_lo, 1)

            for j in range(NPAIR):
                for u in range(2):
                    if u == 0 and G0 + 2 * j + 2 < D0:
                        pass
                    dve.wait_ge(ff_ps, 4 * j + 3 + u)
                    dve.wait_ge(silu_done, 2 * j + u + 1)
                    nc.vector.tensor_tensor(hT[:, 2 * j + u, :], ps[:, 4 * (j % 2) + 2 + u, :], silu_g[:, j % 2, u, :],
                                            ALU.mult).then_inc(h_done, 1)
                    split_lo(G0 + 2 * j + 2 + u)

            for q in range(2 * NDOWN):
                j = q % NDOWN
                dve.wait_ge(hs_hi, q + 1)
                nc.vector.tensor_tensor(h_lo[:, q % 2, :, :], hT[:, 2 * j:2 * j + 2, :],
                                        h_hi[:, q % 2, :, :].bitcast(F32), ALU.subtract).then_inc(hs_lo, 1)
                if q + 2 < 2 * NDOWN:
                    split_lo(D0 + q + 2)
                if NDOWN <= q < NDOWN + TILES:
                    i = q - NDOWN
                    dve.wait_ge(down_done, i + 1)
                    residual(1, i, 0)
                    half_stats(1, i, 0, 2 * TILES + i + 1)
            for i in range(TILES):
                dve.wait_ge(down_done, TILES + i + 1)
                residual(1, i, 1)
                half_stats(1, i, 1, 3 * TILES + i + 1).then_inc(ln_step, 1)
                aggregate(1, i)
                if i >= 1:
                    normalise(1, i - 1)
            normalise(1, TILES - 1)

        @block.gpsimd
        def _(pool):
            g = nc.gpsimd
            step = const_step
            n = [0]

            def link(ins):
                n[0] += 1
                ins.then_inc(step, 1)
                pool.wait_ge(step, n[0])

            link(g.memset(ident[:], 0.0))
            link(g.affine_select(out=ident[:], in_=ident[:], compare_op=ALU.not_equal, fill=1.0, base=0,
                                 pattern=[[-1, P]], channel_multiplier=1))
            pool.nop().then_inc(consts_ready, 1)
            g.memset(mean_w[:], 1.0 / P)
            link(g.iota(dist[:], pattern=[[-1, 512]], base=384, channel_multiplier=1,
                        allow_small_or_imprecise_dtypes=True))
            link(g.tensor_scalar(keep_state[:], dist[:], 0.0, None, ALU.max))
            link(g.tensor_scalar(dist[:], dist[:], -1.0, 0.0, ALU.mult, ALU.max))
            link(g.tensor_tensor(dist[:], dist[:], keep_state[:], ALU.add))
            link(g.memset(keep_state[:], 1.0))
            link(g.memset(keep_state[:].rearrange("p (c t) -> p c t", t=CH)[:, :, 0:1], 0.0))
            link(g.memset(level_mask[:], 1))
            for l, m in enumerate(LEVELS):
                v = level_mask[:, l, :].rearrange("p (b t) -> p b t", t=m)
                link(g.affine_select(out=v, in_=v, compare_op=ALU.is_ge, fill=0.0, base=0,
                                     pattern=[[-2 * m, CH // m], [0, m]], channel_multiplier=1))
                link(g.affine_select(out=v, in_=v, compare_op=ALU.is_ge, fill=0.0, base=m - 1,
                                     pattern=[[2 * m, CH // m], [0, m]], channel_multiplier=-1))
            pool.nop().then_inc(consts_ready, 1)

            pool.wait_ge(lb_step, 6)
            for h in range(HG):
                pool.wait_ge(unit_out, FIRST["hf"] + h + 1)
                g.tensor_scalar(GT[:, h, :], kkT[:, h, :], one_lb[:, h:h + 1], lb[:, h:h + 1], ALU.mult,
                                ALU.add).then_inc(f_done, 1)
                pool.wait_ge(f_done, h + 1)
                g.tensor_scalar(kkT[:, h, :], GT[:, h, :], -1.0, 1.0, ALU.mult, ALU.add).then_inc(kk_done, 1)
            pool.wait_ge(small_out, 2)
            for h in range(HG):
                pool.wait_ge(unit_out, FIRST["hg"] + h + 1)
                g.tensor_scalar(hgT[:, h, :], hgT[:, h, :], norm_g[:, h:h + 1], None, ALU.mult).then_inc(hg_scaled, 1)

            for a in range(HEADS * TILES):
                i = a % 4
                pool.wait_ge(rinv_done, a + 1)
                g.tensor_scalar(probs[:, a % 2, 0:P * (i + 1)], probs[:, a % 2, 0:P * (i + 1)], rinv[:, a:a + 1], None,
                                ALU.mult).then_inc(normed, 1)

            pool.wait_ge(pv_done, HEADS)
            pool.wait_ge(G_done, HG)
            g.memset(AT[:], 0.0).then_inc(A_clear, 1)

            def halves(t, m):
                v = t[:].rearrange("p h (b t) -> p (h b) t", t=2 * m)
                return v[:, :, 0:m], v[:, :, m:2 * m]

            def sub(l):
                m = LEVELS[l]
                if l >= 2:
                    pool.wait_ge(lev_ps, 2 * (l - 1))
                G1, G2 = halves(GT, m)
                e1, e2 = halves(E[l % 2], m)
                ref = GT[:].rearrange("p h (b t) -> p (h b) t", t=2 * m)[:, :, m - 1:m].broadcast_to(
                    [P, HG * SEQ // (2 * m), m])
                g.tensor_tensor(e1, ref, G1, ALU.subtract).then_inc(lev_sub, 1)
                g.tensor_tensor(e2, G2, ref, ALU.subtract).then_inc(lev_sub, 1)

            def mul(l):
                m = LEVELS[l]
                pool.wait_ge(lev_exp, l + 1)
                e1, e2 = halves(E[l % 2], m)
                k1, _ = halves(kkT, m)
                _, q2 = halves(hqT, m)
                g.tensor_tensor(e1, e1, k1, ALU.mult).then_inc(lev_mul, 1)
                g.tensor_tensor(e2, e2, q2, ALU.mult).then_inc(lev_mul, 1)

            sub(0)
            for l in range(len(LEVELS)):
                if l + 1 < len(LEVELS):
                    sub(l + 1)
                mul(l)
            pool.wait_ge(lev_ps, 2 * (len(LEVELS) - 1))
            Gc = GT[:].rearrange("p h (c t) -> p (h c) t", t=CH)
            g.tensor_tensor(E0[:].rearrange("p h (c t) -> p (h c) t", t=CH),
                            Gc[:, :, CH - 1:CH].broadcast_to([P, HG * NCH, CH]), Gc, ALU.subtract).then_inc(kd_sub, 1)
            pool.wait_ge(kd_exp, 1)
            g.tensor_tensor(E0[:], E0[:], kkT[:], ALU.mult).then_inc(kd_mul, 1)
            pool.wait_ge(qg_exp, 1)
            g.tensor_tensor(E1[:], E1[:], hqT[:], ALU.mult).then_inc(qg_mul, 1)

            pool.wait_ge(ln_par, 64)
            for s in range(2):
                t = x1 if s == 0 else y2
                gg, bb = (g1, b1) if s == 0 else (g2, b2)
                for i in range(TILES):
                    k = s * TILES + i
                    pool.wait_ge(ln_norm, k + 1)
                    g.tensor_tensor(t[:, i, :], t[:, i, :], gg[:], ALU.mult).then_inc(ln_g, 1)
                    pool.wait_ge(ln_g, k + 1)
                    g.tensor_tensor(t[:, i, :], t[:, i, :], bb[:], ALU.add).then_inc(ln_b, 1)


_INS = ["x", "w_in", "w_out", "hg_lb_logits", "hg_norm_g", "ln1_g", "ln1_b", "w_gate", "w_up", "w_down",
        "ln2_g", "ln2_b"]


def kernel(**inputs):
    import numpy as np
    from concourse import bacc
    from concourse.bass_utils import run_bass_kernel_spmd

    nc = bacc.Bacc("TRN2", target_bir_lowering=False, num_devices=1)
    arrays, args = {}, []
    for name in _INS:
        a = np.ascontiguousarray(inputs[name])
        arrays[f"in_{name}"] = a
        args.append(nc.dram_tensor(f"in_{name}", a.shape, mybir.dt.from_np(a.dtype), kind="ExternalInput").ap())
    args.append(nc.dram_tensor("out_y", (1, SEQ, D), F32, kind="ExternalOutput").ap())
    build(nc, *args)
    return run_bass_kernel_spmd(nc, [arrays], core_ids=[0]).results[0]["out_y"]
```

```python
from contextlib import ExitStack

import concourse.bass as bass
from concourse import mybir

F32 = mybir.dt.float32
F32R = mybir.dt.float32r
I32 = mybir.dt.int32
ALU = mybir.AluOpType
ACT = mybir.ActivationFunctionType

P = 128
SEQ, D = 512, 1024
TILES = SEQ // P
KT = D // P
HEADS, DH = 8, 64
TOPK = 128
HG = 4
CH = 64
NCH = SEQ // CH
FF = 2816
FT = FF // P
ALPHA = 2.0 ** 0.25
LN_EPS, RMS_EPS = 1e-5, 1e-6
IDX_SCALE = (64 ** -0.5) * (8 ** -0.5)
NEG = -3.0e38
TAKEN = -3.4e38
FAR = -1.0e30
LEVELS = [32, 16, 8, 4, 2, 1]

IN_SLABS = [("iq", 1536, 256), ("iq", 1792, 256), ("ik", 2048, 72),
            ("hf", 2632, 256), ("hf", 2888, 256), ("hq", 2120, 256), ("hq", 2376, 256),
            ("hi", 3144, 256), ("hi", 3400, 256), ("hg", 3656, 256), ("hg", 3912, 256),
            ("dk", 512, 256), ("dk", 768, 256), ("dq", 0, 256), ("dq", 256, 256),
            ("dv", 1024, 256), ("dv", 1280, 256)]
N_IN = len(IN_SLABS)
OUT_SLABS = [(4, 0), (0, 0), (4, 1), (0, 1)]
W0 = N_IN
G0 = W0 + len(OUT_SLABS)
NPAIR = FT // 2
D0 = G0 + 2 * NPAIR
DOWN_ROWS = [(half, f) for half in range(2) for f in range(FT)]
NDOWN = len(DOWN_ROWS) // 4

UNITS = [(n, u, kind) for n, (kind, _, w) in enumerate(IN_SLABS) for u in range(2 if w == 256 else 1)]
NU = len(UNITS)
FIRST = {kind: min(j for j, v in enumerate(UNITS) if v[2] == kind) for _, _, kind in UNITS}
INDEX_AT = FIRST["hf"] + 1
TURN_TILES = (3, 2, 1)
SELECT_STEPS = [(r, op, i) for r in range(TOPK // 8) for op in ("max", "take") for i in TURN_TILES]
SELECT_A_UNIT = 4
DIAG_AT = 14
LEVEL_AT = [15 + 2 * l for l in range(len(LEVELS))]
KD_AT = 27
U_AT = [29, 31]
STEPS = HEADS * TILES
LAG = 4
NPROB = 5
QK_BANKS = (0, 1, 4, 5)


def build(nc, x, w_in, w_out, hg_lb_logits, hg_norm_g, ln1_g, ln1_b, w_gate, w_up, w_down,
          ln2_g, ln2_b, out):
    x_d = x.rearrange("a (i p) d -> p (a i) d", p=P)
    out_d = out.rearrange("a (i p) d -> p (a i) d", p=P)
    win_d = w_in.rearrange("a (k p) n -> p (a k) n", p=P)
    wout_d = w_out.rearrange("a (k p) n -> p (a k) n", p=P)
    gate_d = w_gate.rearrange("a (k p) n -> p (a k) n", p=P)
    up_d = w_up.rearrange("a (k p) n -> p (a k) n", p=P)
    down_d = w_down.rearrange("a (f p) n -> p (a f) n", p=P)

    with ExitStack() as ctx:
        def sem(name):
            return ctx.enter_context(nc.semaphore(name))

        top = [16512]

        def at(name, shape, dt, offset):
            return nc.alloc_sbuf_tensor_at(name, shape, dt, offset=offset)

        def keep(name, shape, dt=F32):
            size = 4
            for s in shape[1:]:
                size *= s
            t = at(name, shape, dt, top[0])
            top[0] += (size + 31) // 32 * 32
            assert top[0] <= 229344, (name, top[0])
            return t

        ctx.enter_context(nc.sbuf_tensor("arena", [P, 52000], F32))
        ident = keep("ident", [P, P])
        mean_w = keep("mean_w", [P, P])
        level_mask = keep("level_mask", [P, len(LEVELS), CH], I32)
        dist = keep("dist", [P, 512])
        keep_state = keep("keep_state", [P, 512])
        small = keep("small", [P, P])
        small_t = keep("small_t", [P, 28])
        lb_l = small_t[:, 0:8].rearrange("p (l h) -> p l h", h=HG)
        norm_g, g1_t, b1_t = small_t[:, 8:12], small_t[:, 12:20], small_t[:, 20:28]
        lb_e = keep("lb_e", [P, 2, HG])
        lb_m = keep("lb_m", [P, HG])
        lb = keep("lb", [P, HG])
        one_lb = keep("one_lb", [P, HG])
        iw_n = keep("iw_n", [P, TILES, HEADS])
        top8 = keep("top8", [P, TILES, 8])
        nmax = keep("nmax", [P, STEPS])
        rsum = keep("rsum", [P, STEPS])
        rinv = keep("rinv", [P, STEPS])
        chunk_decay = keep("chunk_decay", [P, HG, NCH])
        stats = keep("stats", [P, 2 * TILES, 2, 6])
        moments = keep("moments", [P, 2 * TILES, 2])
        spread = keep("spread", [P, 2 * TILES])
        shift = keep("shift", [P, 2 * TILES])
        eps_ln = keep("eps_ln", [P, 1])
        eps_rms = keep("eps_rms", [P, 1])

        xT_hi = keep("xT_hi", [P, KT, SEQ], F32R)
        xT_lo = keep("xT_lo", [P, KT, SEQ], F32R)
        w_hi = keep("w_hi", [P, 2, 2048], F32R)
        w_lo = keep("w_lo", [P, 2, 2048], F32R)
        raw = keep("raw", [P, 2, 2048])
        zone = top[0]
        hqT = keep("hqT", [P, HG, SEQ])
        hvN = keep("hvN", [P, TILES, 512])
        E0 = keep("E0", [P, HG, SEQ])
        E1 = keep("E1", [P, HG, SEQ])
        GT = keep("GT", [P, HG, SEQ])
        kkT = keep("kkT", [P, HG, SEQ])
        hgT = keep("hgT", [P, HG, SEQ])
        AT = keep("AT", [P, HG * TILES, P])
        kdN = keep("kdN", [P, HG * TILES, P])
        sq = keep("sq", [P, HG, SEQ])
        qT = keep("qT", [P, 4, SEQ])
        kT = keep("kT", [P, 4, SEQ])
        vN = keep("vN", [P, TILES, 512])
        SC0 = {1: 0, 2: 256, 3: 640}
        M0 = {0: 0, 1: 128, 2: 384, 3: 768}
        mask = keep("mask", [P, 1280])
        score = at("score", [P, 1152], F32, top[0])
        probs = keep("probs", [P, NPROB, SEQ])
        o = zone + 16384
        iqT = at("iqT", [P, 4, SEQ], F32, o)
        ikT = at("ikT", [P, SEQ], F32, o + 8192)
        rel = at("rel", [P, 2, SEQ], F32, o + 10240)
        iwT = at("iwT", [P, SEQ], F32, o + 14336)
        state = at("state", [P, HG, NCH - 1, P], F32, o)
        probsT = at("probsT", [P, 2, TILES, SEQ], F32, zone + 32768)
        diag_inv = at("diag_inv", [P, 4, P], F32, zone + 57344)
        oT = at("oT", [P, HG, SEQ], F32, zone + 65536)
        vtmp = at("vtmp", [P, 2, SEQ], F32, zone + 73728)
        x_in = at("x_in", [P, TILES, D], F32, zone + 81920)
        x1 = at("x1", [P, TILES, D], F32, zone)
        g1 = at("g1", [P, D], F32, o)
        b1 = at("b1", [P, D], F32, o + 4096)
        g2 = at("g2", [P, D], F32, o + 8192)
        b2 = at("b2", [P, D], F32, o + 12288)
        x1T_v = at("x1T_v", [P, 2, SEQ], F32, zone + 32768)
        silu_g = at("silu_g", [P, 2, 2, SEQ], F32, zone + 32768)
        hT = at("hT", [P, FT, SEQ], F32, zone + 40960)
        o = zone + 40960 + FT * 2048
        x1n = at("x1n", [P, TILES, D], F32, o - 16384)
        h_hi = at("h_hi", [P, 2, 4, SEQ], F32R, o)
        h_lo = at("h_lo", [P, 2, 4, SEQ], F32R, o + 16384)
        assert o + 32768 <= 229344

        ps = ctx.enter_context(nc.psum_tensor("ps", [P, 8, 512], F32))

        x_loaded = [sem(f"x_loaded{i}") for i in range(TILES)]
        small_loaded, small_turned, small_out = sem("small_loaded"), sem("small_turned"), sem("small_out")
        raw_loaded = [sem(f"raw_loaded{i}") for i in range(2)]
        hi_done, lo_done = sem("hi_done"), sem("lo_done")
        out_used, down_used = sem("out_used"), sem("down_used")
        const_step, ident_ready, consts_ready = sem("const_step"), sem("ident_ready"), sem("consts_ready")
        xT_ps, xT_hi_done, xT_lo_done = sem("xT_ps"), sem("xT_hi_done"), sem("xT_lo_done")
        unit_done, unit_out = sem("unit_done"), sem("unit_out")
        vturn, vturn_out = sem("vturn"), sem("vturn_out")
        iw_turned, iw_ready = sem("iw_turned"), sem("iw_ready")
        idx_done, rel_done, acc_done = sem("idx_done"), sem("rel_done"), sem("acc_done")
        topk_step, mask_ready = sem("topk_step"), sem("mask_ready")
        qk_done, biased, masked = sem("qk_done"), sem("biased"), sem("masked")
        exp_done, rinv_done, diag_ready = sem("exp_done"), sem("rinv_done"), sem("diag_ready")
        pT_done, pT_out = sem("pT_done"), sem("pT_out")
        pv_done, a_hi_done, a_lo_done = sem("pv_done"), sem("a_hi_done"), sem("a_lo_done")
        lb_step, lb_exp = sem("lb_step"), sem("lb_exp")
        f_done, kk_done, ln_done, G_done = sem("f_done"), sem("kk_done"), sem("ln_done"), sem("G_done")
        hg_scaled = sem("hg_scaled")
        A_clear, A_step = sem("A_clear"), sem("A_step")
        lev_sub, lev_exp, lev_mul, lev_ps = sem("lev_sub"), sem("lev_exp"), sem("lev_mul"), sem("lev_ps")
        diag_ps = sem("diag_ps")
        kd_sub, kd_exp, kd_mul = sem("kd_sub"), sem("kd_exp"), sem("kd_mul")
        kd_ps, kd_out = sem("kd_ps"), sem("kd_out")
        qg_exp, qg_mul, cd_exp = sem("qg_exp"), sem("qg_mul"), sem("cd_exp")
        U_ps, state_step = sem("U_ps"), sem("state_step")
        o_ps, o_out, sq_done, ms_ps, rms_ln, rms_done = (
            sem(s) for s in ("o_ps", "o_out", "sq_done", "ms_ps", "rms_ln", "rms_done"))
        r_a, r_b, r_hi, r_lo = sem("r_a"), sem("r_b"), sem("r_hi"), sem("r_lo")
        x1_loaded = [sem(f"x1_loaded{i}") for i in range(TILES)]
        par_loaded = sem("par_loaded")
        mix_done, res_done, ln_step, ln_root, ln_inv, ln_shift, ln_norm = (
            sem(s) for s in ("mix_done", "res_done", "ln_step", "ln_root", "ln_inv", "ln_shift", "ln_norm"))
        ln_g, ln_b, x1_g, mix_half = sem("ln_g"), sem("ln_b"), sem("x1_g"), sem("mix_half")
        x1T_ps, x1T_v_done, x1T_hi, x1T_lo = sem("x1T_ps"), sem("x1T_v_done"), sem("x1T_hi"), sem("x1T_lo")
        ff_ps, silu_done, h_done = sem("ff_ps"), sem("silu_done"), sem("h_done")
        hs_hi, hs_lo, down_done = sem("hs_hi"), sem("hs_lo"), sem("down_done")
        stored = sem("stored")

        block = ctx.enter_context(nc.Block())

        def size_of(n):
            return KT * IN_SLABS[n][2] if n < N_IN else 2048

        def wait_used(eng, n):
            if n < N_IN:
                eng.wait_ge(unit_done, sum(1 for m, _, _ in UNITS if m <= n))
            elif n < G0 - 1:
                eng.wait_ge(out_used, n - W0 + 1)
            elif n < G0:
                eng.wait_ge(mix_done, TILES)
            elif n < D0:
                eng.wait_ge(ff_ps, 2 * (n - G0) + 2)
            else:
                eng.wait_ge(down_used, n - D0 + 1)

        def sc(i):
            return score[:, SC0[i]:SC0[i] + P * (i + 1)]

        def runs(q):
            half, f = DOWN_ROWS[4 * q]
            a = min(4, FT - f)
            return [((0, a), (f, f + a))] + ([((a, 4), (0, 4 - a))] if a < 4 else [])

        @block.sync
        def _(sp):
            def load(n, parts):
                if n >= 2:
                    sp.wait_ge(lo_done, n - 1)
                for dst, src in parts:
                    sp.dma_start(dst, src).then_inc(raw_loaded[n % 2], 16)

            def load_in(n):
                _, c, w = IN_SLABS[n]
                load(n, [(raw[:, n % 2, 0:KT * w].rearrange("p (k n) -> p k n", k=KT), win_d[:, :, c:c + w])])

            def load_out(q):
                k0, half = OUT_SLABS[q]
                load(W0 + q, [(raw[:, (W0 + q) % 2, :].rearrange("p (k n) -> p k n", k=4),
                               wout_d[:, k0:k0 + 4, half * 512:half * 512 + 512])])

            for i in range(TILES):
                sp.dma_start(x_in[:, i, :], x_d[:, i, :]).then_inc(x_loaded[i], 16)
            for n in range(N_IN):
                load_in(n)
            load_out(0)
            load_out(1)
            sp.wait_ge(o_ps, HG)
            for i in range(TILES):
                sp.dma_start(x1[:, i, :], x_d[:, i, :]).then_inc(x1_loaded[i], 16)
            for t, v in ((g1, ln1_g), (b1, ln1_b), (g2, ln2_g), (b2, ln2_b)):
                sp.dma_start(t[:], v.partition_broadcast(P).rearrange("p a d -> p (a d)")).then_inc(par_loaded, 16)
            load_out(2)
            load_out(3)
            for j in range(NPAIR):
                for v, w_d in enumerate((gate_d, up_d)):
                    n = G0 + 2 * j + v
                    load(n, [(raw[:, n % 2, :].rearrange("p (k n) -> p k n", k=KT), w_d[:, :, 256 * j:256 * j + 256])])
            for q in range(NDOWN):
                n = D0 + q
                half, f = DOWN_ROWS[4 * q]
                v = raw[:, n % 2, :].rearrange("p (k n) -> p k n", k=4)
                a = min(4, FT - f)
                parts = [(v[:, 0:a, :], down_d[:, f:f + a, half * 512:half * 512 + 512])]
                if a < 4:
                    parts.append((v[:, a:4, :], down_d[:, 0:4 - a, 512:1024]))
                load(n, parts)
            for i in range(TILES):
                sp.wait_ge(ln_b, TILES + i + 1)
                sp.dma_start(out_d[:, i, :], x1[:, i, :]).then_inc(stored, 16)
            sp.wait_ge(stored, 16 * TILES)

        @block.tensor
        def _(pe):
            mm, turn = nc.tensor.matmul, nc.tensor.transpose

            def three(o, a_hi, a_lo, b_hi, b_lo, first, end):
                mm(o, a_hi, b_hi, start=first, stop=False)
                mm(o, a_hi, b_lo, start=False, stop=False)
                return mm(o, a_lo, b_hi, start=False, stop=end)

            pe.wait_ge(ident_ready, 1)
            pe.wait_ge(small_loaded, 64)
            turn(ps[:, 3, 0:28], small[0:28, :], ident[0:28, 0:28]).then_inc(small_turned, 1)
            for kt in range(KT):
                if kt >= 4:
                    pe.wait_ge(xT_lo_done, kt - 3)
                for i in range(TILES):
                    if kt == 0:
                        pe.wait_ge(x_loaded[i], 16)
                    last = turn(ps[:, 4 + kt % 4, i * P:(i + 1) * P], x_in[:, i, kt * P:(kt + 1) * P], ident[:])
                last.then_inc(xT_ps, 1)

            def product(o, slab, u, m, w, end_sem, wait_x=None):
                for kt in range(KT):
                    if wait_x is not None:
                        pe.wait_ge(wait_x, kt + 1)
                    c = kt * w + u * P
                    last = three(o, w_hi[:, slab, c:c + m], w_lo[:, slab, c:c + m], xT_hi[:, kt, :], xT_lo[:, kt, :],
                                 kt == 0, kt == KT - 1)
                last.then_inc(end_sem, 1)

            def unit(j):
                n, u, kind = UNITS[j]
                w = IN_SLABS[n][2]
                m = min(w, P)
                if u == 0:
                    pe.wait_ge(lo_done, n + 1)
                if j >= 2:
                    pe.wait_ge(unit_out, j - 1)
                product(ps[0:m, j % 2, :], n % 2, u, m, w, unit_done, xT_lo_done if j == 0 else None)

            def turn_v(t):
                pe.wait_ge(unit_out, (FIRST["hi"] + t if t < 4 else FIRST["dv"] + t - 4) + 1)
                if t >= 2:
                    pe.wait_ge(vturn_out, t - 1)
                for i in range(TILES):
                    last = turn(ps[:, 4 + t % 2, i * P:(i + 1) * P], vtmp[:, t % 2, i * P:(i + 1) * P], ident[:])
                last.then_inc(vturn, 1)

            def index():
                pe.wait_ge(unit_out, FIRST["ik"] + 1)
                for i in range(TILES):
                    last = turn(ps[:, 4, i * 8:i * 8 + 8], iwT[0:8, i * P:(i + 1) * P], ident[0:8, 0:8])
                last.then_inc(iw_turned, 1)
                for j in range(HEADS * len(TURN_TILES)):
                    h, i = j // 3, TURN_TILES[j % 3]
                    a = 64 * (h % 2)
                    if j >= 2:
                        pe.wait_ge(rel_done, j - 1)
                    mm(ps[:, 2 + j % 2, 0:P * (i + 1)], iqT[a:a + 64, h // 2, i * P:(i + 1) * P],
                       ikT[a:a + 64, 0:P * (i + 1)], start=True, stop=True).then_inc(idx_done, 1)

            def pair(t, p):
                return t[:, p // 4, (p % 4) * P:(p % 4 + 1) * P]

            def diagonal():
                pe.wait_ge(unit_out, FIRST["hq"] + HG)
                pe.wait_ge(kk_done, HG)
                pe.wait_ge(rel_done, HEADS * len(TURN_TILES))
                for p in range(HG * TILES):
                    bank = (6, 7, 2, 3)[p // 4]
                    last = mm(ps[:, bank, (p % 4) * P:(p % 4 + 1) * P], pair(kkT, p), pair(hqT, p),
                              start=(p % 4 == 0), stop=(p % 4 == 3), skip_group_check=True)
                    if p % 4 == 3:
                        last.then_inc(diag_ps, 1)

            def level(l):
                m = LEVELS[l]
                pe.wait_ge(lev_mul, 2 * (l + 1))
                pe.wait_ge(A_step, 4 + 2 * l)
                for p in range(HG * TILES):
                    X = pair(E1 if l % 2 else E0, p)
                    second = X.rearrange("p (b t) -> p b t", t=2 * m)[:, :, m:2 * m]
                    o = ps[:, 2 + p // 8, (p % 8) * CH:(p % 8 + 1) * CH].rearrange("p (b t) -> p b t", t=m)
                    last = mm(o, X, second, start=(p % 8 == 0), stop=(p % 8 == 7), skip_group_check=True)
                    if p % 8 == 7:
                        last.then_inc(lev_ps, 1)

            def turn_kd():
                pe.wait_ge(kd_mul, 1)
                pe.wait_ge(A_step, 4 + 2 * len(LEVELS))
                for p in range(HG * TILES):
                    bank = (6, 7, 2, 3)[p // 4]
                    last = turn(ps[:, bank, (p % 4) * P:(p % 4 + 1) * P], pair(kkT, p), ident[:])
                    if p % 4 == 3:
                        last.then_inc(kd_ps, 1)

            def chunk_sums(h0):
                pe.wait_ge(kd_out, HG)
                if h0:
                    pe.wait_ge(state_step, 2 * (NCH - 1))
                pe.wait_ge(vturn_out, HG)
                for h in (h0, h0 + 1):
                    for c in range(NCH - 1):
                        b, f = CH * (c % 2), (c // 2) * P
                        last = mm(ps[:, (2, 6)[h % 2] + c % 2, f:f + P], kdN[b:b + CH, 4 * h + c // 2, :],
                                  hvN[b:b + CH, c // 2, h * P:(h + 1) * P], start=(c < 2), stop=(c >= NCH - 3),
                                  skip_group_check=True)
                last.then_inc(U_ps, 1)

            def outputs():
                pe.wait_ge(qg_mul, 1)
                pe.wait_ge(vturn_out, 2 * HG)
                pe.wait_ge(state_step, 4 * (NCH - 1))
                for h in range(HG):
                    bank = 4 + h
                    for p in range(TILES):
                        mm(ps[:, bank, p * P:(p + 1) * P], hvN[:, p, h * P:(h + 1) * P], AT[:, 4 * h + p, :],
                           start=(p == 0), stop=False, skip_group_check=True)
                    for c in range(1, NCH):
                        last = mm(ps[:, bank, c * CH:(c + 1) * CH], state[:, h, c - 1, :], hqT[:, h, c * CH:(c + 1) * CH],
                                  start=False, stop=(c == NCH - 1), skip_group_check=True)
                    last.then_inc(o_ps, 1)

            for j in range(NU):
                unit(j)
                if 1 <= j - FIRST["hi"] <= HG:
                    turn_v(j - 1 - FIRST["hi"])
                if 1 <= j - FIRST["dv"] <= HG:
                    turn_v(j - 1 - FIRST["dv"] + HG)
                if j == INDEX_AT:
                    index()
                if j == DIAG_AT:
                    diagonal()
                if j in LEVEL_AT:
                    level(LEVEL_AT.index(j))
                if j == KD_AT:
                    turn_kd()
                if j in U_AT:
                    chunk_sums(2 * U_AT.index(j))
            def qk(a):
                h, i = a // 4, a % 4
                b = 64 * (h % 2)
                if a == 0:
                    pe.wait_ge(unit_out, NU)
                if a == 2:
                    pe.wait_ge(rms_ln, HG)
                if a >= 4:
                    pe.wait_ge(biased, a - 3)
                mm(ps[:, QK_BANKS[a % 4], 0:P * (i + 1)], qT[b:b + 64, h // 2, i * P:(i + 1) * P],
                   kT[b:b + 64, h // 2, 0:P * (i + 1)], start=True, stop=True).then_inc(qk_done, 1)

            def turn_p(a):
                i = a % 4
                pe.wait_ge(diag_ready, a + 1)
                if a == 0:
                    pe.wait_ge(sq_done, HG)
                    pe.wait_ge(o_out, HG)
                if a >= 2:
                    pe.wait_ge(pT_out, a - 1)
                for j in range(i + 1):
                    last = mm(ps[:, 6 + a % 2, j * P:(j + 1) * P], probs[:, a % NPROB, j * P:(j + 1) * P],
                              diag_inv[:, a % 4, :], start=(j == 0), stop=(j == i), skip_group_check=True)
                last.then_inc(pT_done, 1)

            def pv(h):
                pe.wait_ge(pT_out, 4 * h + 4)
                g, b = h // 2, 64 * (h % 2)
                if h >= 4:
                    pe.wait_ge(a_lo_done, g - 1)
                for j in range(TILES):
                    last = mm(ps[b:b + 64, 2 + g % 2, j * P:SEQ], vN[:, j, h * DH:(h + 1) * DH],
                              probsT[:, h % 2, j, j * P:SEQ], start=(j == 0), stop=(j == TILES - 1))
                last.then_inc(pv_done, 1)

            turn_v(2 * HG - 1)
            qk(0)
            qk(1)
            outputs()
            for h in range(HG):
                pe.wait_ge(sq_done, h + 1)
                if h >= 2:
                    pe.wait_ge(o_out, h - 1)
                mm(ps[:, 2 + h, :], mean_w[:], sq[:, h, :], start=True, stop=True).then_inc(ms_ps, 1)
            for s in range(2, STEPS + LAG):
                if s < STEPS:
                    qk(s)
                if s >= LAG:
                    turn_p(s - LAG)
                if s >= LAG + 5 and (s - LAG) % 4 == 1 and (s - LAG) // 4 <= HEADS - 1:
                    pv((s - LAG) // 4 - 1)

            def mix(q, rows=range(4)):
                n = W0 + q
                k0, half = OUT_SLABS[q]
                pe.wait_ge(lo_done, n + 1)
                order = [(kk, i) for kk in rows for i in range(TILES)]
                if q == 3:
                    order = [(kk, i) for i in range(TILES) for kk in range(4)]
                for kk, i in order:
                    c, r = slice(i * P, (i + 1) * P), slice(kk * 512, (kk + 1) * 512)
                    last = three(ps[:, (4 if half == 0 else 0) + i, :], xT_hi[:, k0 + kk, c], xT_lo[:, k0 + kk, c],
                                 w_hi[:, n % 2, r], w_lo[:, n % 2, r], k0 == 4 and kk == 0, k0 == 0 and kk == 3)
                    if q == 1 and kk == 3 and i < TILES - 1 or q == 3 and kk == 3:
                        last.then_inc(mix_half if q == 1 else mix_done, 1)
                if q < 3 and rows[-1] == 3:
                    last.then_inc(out_used, 1)

            pe.wait_ge(pT_out, STEPS)
            pe.wait_ge(r_lo, HG)
            mix(0, range(2))
            pv(HEADS - 1)
            mix(0, range(2, 4))
            pe.wait_ge(a_lo_done, 4)
            for q in (1, 2, 3):
                mix(q)

            for i in range(TILES):
                pe.wait_ge(ln_norm, i + 1)
                for kt in range(4):
                    last = turn(ps[:, 4 + kt, i * P:(i + 1) * P], x1n[:, i, kt * P:(kt + 1) * P], ident[:])
                    if i == TILES - 1:
                        last.then_inc(x1T_ps, 1)
            pe.wait_ge(res_done, 2 * TILES)
            for kt in range(4, KT):
                for i in range(TILES):
                    last = turn(ps[:, kt - 4, i * P:(i + 1) * P], x1n[:, i, kt * P:(kt + 1) * P], ident[:])
                last.then_inc(x1T_ps, 1)

            for j in range(NPAIR):
                for v in range(2):
                    n = G0 + 2 * j + v
                    pe.wait_ge(lo_done, n + 1)
                    if j >= 2:
                        pe.wait_ge(h_done, 2 * (j - 1))
                    for u in range(2):
                        if j == 0 and v + u == 1:
                            pe.wait_ge(x1T_lo, KT)
                        product(ps[:, (0 if j % 2 else 4) + 2 * v + u, :], n % 2, u, P, 256, ff_ps,
                                x1T_lo if j == v == u == 0 else None)

            for q in range(NDOWN):
                n = D0 + q
                pe.wait_ge(lo_done, n + 1)
                pe.wait_ge(hs_lo, q + 1)
                if q == 0:
                    pe.wait_ge(h_done, 2 * NPAIR)
                order = [(kk, i) for kk in range(4) for i in range(TILES)]
                if q == NDOWN - 1:
                    order = [(kk, i) for i in range(TILES) for kk in range(4)]
                for kk, i in order:
                    half, f = DOWN_ROWS[4 * q + kk]
                    c, r = slice(i * P, (i + 1) * P), slice(kk * 512, (kk + 1) * 512)
                    last = three(ps[:, 4 * half + i, :], h_hi[:, q % 2, kk, c], h_lo[:, q % 2, kk, c],
                                 w_hi[:, n % 2, r], w_lo[:, n % 2, r], f == 0, f == FT - 1)
                    if f == FT - 1:
                        last.then_inc(down_done, 1)
                if q < NDOWN - 1:
                    last.then_inc(down_used, 1)

        @block.scalar
        def _(act):
            def cp(o, i, scale=1.0):
                return nc.scalar.activation(o, i, ACT.Copy, scale=scale)

            arrived = [0, 0]

            def split_hi(n):
                arrived[n % 2] += 32 if (n >= D0 and DOWN_ROWS[4 * (n - D0)][1] + 4 > FT) else 16
                act.wait_ge(raw_loaded[n % 2], arrived[n % 2])
                if n >= 2:
                    wait_used(act, n - 2)
                size = size_of(n)
                cp(w_hi[:, n % 2, 0:size], raw[:, n % 2, 0:size]).then_inc(hi_done, 1)

            act.dma_start(small[0:8, :], hg_lb_logits.rearrange("l (h k) -> (l h) k", k=P)).then_inc(small_loaded, 16)
            act.dma_start(small[8:12, :], hg_norm_g.rearrange("a (h v) -> (a h) v", v=P)).then_inc(small_loaded, 16)
            act.dma_start(small[12:20, :], ln1_g.rearrange("a (h v) -> (a h) v", v=P)).then_inc(small_loaded, 16)
            act.dma_start(small[20:28, :], ln1_b.rearrange("a (h v) -> (a h) v", v=P)).then_inc(small_loaded, 16)
            act.wait_ge(lb_step, 2)
            nc.scalar.activation(lb_e[:], lb_e[:], ACT.Exp).then_inc(lb_exp, 1)
            for kt in range(KT):
                act.wait_ge(xT_ps, kt + 1)
                cp(xT_hi[:, kt, :], ps[:, 4 + kt % 4, :]).then_inc(xT_hi_done, 1)
                if kt == 3:
                    split_hi(0)
            split_hi(1)

            def out_of(j):
                n, u, kind = UNITS[j]
                act.wait_ge(unit_done, j + 1)
                g = j - FIRST[kind]
                src = ps[:, j % 2, :]
                if kind == "iq":
                    cp(iqT[:, g, :], src).then_inc(unit_out, 1)
                elif kind == "ik":
                    cp(ikT[0:64, :], ps[0:64, j % 2, :])
                    cp(ikT[64:128, :], ps[0:64, j % 2, :])
                    cp(iwT[0:8, :], ps[64:72, j % 2, :]).then_inc(unit_out, 1)
                elif kind == "hf":
                    nc.scalar.activation(kkT[:, g, :], src, ACT.Sigmoid).then_inc(unit_out, 1)
                elif kind == "hq":
                    cp(hqT[:, g, :], src).then_inc(unit_out, 1)
                elif kind in ("hi", "dv"):
                    t = g + (HG if kind == "dv" else 0)
                    if t >= 2:
                        act.wait_ge(vturn, t - 1)
                    cp(vtmp[:, t % 2, :], src).then_inc(unit_out, 1)
                elif kind == "hg":
                    nc.scalar.activation(hgT[:, g, :], src, ACT.Silu).then_inc(unit_out, 1)
                elif kind == "dk":
                    cp(kT[:, g, :], src).then_inc(unit_out, 1)
                else:
                    cp(qT[:, g, :], src, DH ** -0.5).then_inc(unit_out, 1)

            def turned_v(t):
                act.wait_ge(vturn, t + 1)
                dst, g = (hvN, t) if t < HG else (vN, t - HG)
                cp(dst[:, :, g * P:(g + 1) * P], ps[:, 4 + t % 2, :].rearrange("p (i f) -> p i f", i=TILES)
                   ).then_inc(vturn_out, 1)

            def relus():
                act.wait_ge(iw_turned, 1)
                cp(iw_n[:].rearrange("p i h -> p (i h)"), ps[:, 4, 0:32], IDX_SCALE).then_inc(iw_ready, 1)
                for j in range(HEADS * len(TURN_TILES)):
                    i = TURN_TILES[j % 3]
                    act.wait_ge(idx_done, j + 1)
                    if j >= 2:
                        act.wait_ge(acc_done, j - 1)
                    nc.scalar.activation(rel[:, j % 2, 0:P * (i + 1)], ps[:, 2 + j % 2, 0:P * (i + 1)],
                                         ACT.Relu).then_inc(rel_done, 1)

            def level_exp(l):
                e = E1 if l % 2 else E0
                act.wait_ge(lev_sub, 2 * (l + 1))
                nc.scalar.activation(e[:], e[:], ACT.Exp).then_inc(lev_exp, 1)

            def late_exps(part):
                if part == 0:
                    nc.scalar.activation(chunk_decay[:], GT[:].rearrange("p h (c t) -> p h c t", t=CH)[:, :, :, CH - 1],
                                         ACT.Exp).then_inc(cd_exp, 1)
                    act.wait_ge(kd_sub, 1)
                    nc.scalar.activation(E0[:], E0[:], ACT.Exp).then_inc(kd_exp, 1)
                else:
                    act.wait_ge(lev_ps, 2 * len(LEVELS))
                    nc.scalar.activation(E1[:], GT[:], ACT.Exp).then_inc(qg_exp, 1)

            def kd_turned():
                for h in range(HG):
                    act.wait_ge(kd_ps, h + 1)
                    cp(kdN[:, 4 * h:4 * h + 4, :], ps[:, (6, 7, 2, 3)[h], :].rearrange("p (a k) -> p a k", k=P)
                       ).then_inc(kd_out, 1)

            for j in range(NU):
                n, u, kind = UNITS[j]
                out_of(j)
                if 1 <= j - FIRST["hi"] <= HG:
                    turned_v(j - 1 - FIRST["hi"])
                if 1 <= j - FIRST["dv"] <= HG:
                    turned_v(j - 1 - FIRST["dv"] + HG)
                if u == 1 or kind == "ik":
                    split_hi(n + 2)
                if j == FIRST["hq"]:
                    for g in range(HG):
                        act.wait_ge(kk_done, g + 1)
                        nc.scalar.activation(GT[:, g, :], GT[:, g, :], ACT.Ln).then_inc(ln_done, 1)
                if j == INDEX_AT:
                    relus()
                if j + 3 in LEVEL_AT:
                    level_exp(LEVEL_AT.index(j + 3))
                if j == LEVEL_AT[-1]:
                    late_exps(0)
                if j == LEVEL_AT[-1] + 1:
                    late_exps(1)
                if j == KD_AT:
                    kd_turned()
            turned_v(2 * HG - 1)
            for h in range(HG):
                act.wait_ge(o_ps, h + 1)
                if h == 0:
                    act.wait_ge(vturn_out, 2 * HG)
                nc.scalar.activation(sq[:, h, :], ps[:, 4 + h, :], ACT.Square).then_inc(sq_done, 1)
            for h in range(HG):
                act.wait_ge(ms_ps, h + 1)
                nc.scalar.activation(sq[:, h, :], ps[:, 2 + h, :], ACT.Ln, bias=eps_rms[:, 0:1]).then_inc(rms_ln, 1)
            for h in range(HG):
                act.wait_ge(rms_ln, h + 1)
                nc.scalar.activation(sq[:, h, :], sq[:, h, :], ACT.Exp, scale=-0.5).then_inc(rms_done, 1)

            def exps(a):
                i = a % 4
                pr = probs[:, a % NPROB, 0:P * (i + 1)]
                act.wait_ge(masked, a + 1)
                nc.scalar.activation(pr, pr, ACT.Exp, bias=nmax[:, a:a + 1], scale=-1.0,
                                     accum_out=rsum[:, a:a + 1]).then_inc(exp_done, 1)

            def turned_p(a):
                h, i = a // 4, a % 4
                act.wait_ge(pT_done, a + 1)
                if a == 0:
                    act.wait_ge(qg_exp, 1)
                if h >= 2 and i == 0:
                    act.wait_ge(pv_done, h - 1)
                cp(probsT[:, h % 2, 0:i + 1, i * P:(i + 1) * P],
                   ps[:, 6 + a % 2, 0:P * (i + 1)].rearrange("p (j q) -> p j q", q=P)).then_inc(pT_out, 1)

            def a_high(g):
                act.wait_ge(pv_done, 2 * g + 2)
                cp(xT_hi[:, g, :], ps[:, 2 + g % 2, :]).then_inc(a_hi_done, 1)

            def r_high(h):
                act.wait_ge(r_b, h + 1)
                cp(xT_hi[:, 4 + h, :], hgT[:, h, :]).then_inc(r_hi, 1)

            for s in range(STEPS + LAG):
                if s < STEPS:
                    exps(s)
                if s >= LAG:
                    turned_p(s - LAG)
                if s in (9, 10, 11, 12):
                    r_high(s - 9)
                if s - LAG - 10 in (0, 8, 16):
                    a_high((s - LAG - 10) // 8)
            a_high(3)
            split_hi(W0 + 2)
            split_hi(W0 + 3)
            split_hi(G0)

            def root(s, i):
                k = s * TILES + i
                act.wait_ge(ln_step, 2 * k + 2)
                nc.scalar.activation(spread[:, k:k + 1], moments[:, k, 1:2], ACT.Sqrt, bias=eps_ln[:, 0:1]
                                     ).then_inc(ln_root, 1)

            def normalise(s, i):
                k = s * TILES + i
                act.wait_ge(ln_shift, k + 1)
                dst = x1n if s == 0 else x1
                nc.scalar.activation(dst[:, i, :], x1[:, i, :], ACT.Identity, scale=spread[:, k:k + 1],
                                     bias=shift[:, k:k + 1]).then_inc(ln_norm, 1)

            for i in range(TILES):
                root(0, i)
                normalise(0, i)
            split_hi(G0 + 1)
            for kt in range(KT):
                act.wait_ge(x1T_ps, kt + 1)
                if kt >= 2:
                    act.wait_ge(x1T_lo, kt - 1)
                nc.scalar.activation(x1T_v[:, kt % 2, :], ps[:, 4 + kt if kt < 4 else kt - 4, :], ACT.Identity,
                                     scale=g1_t[:, kt:kt + 1], bias=b1_t[:, kt:kt + 1]).then_inc(x1T_v_done, 1)

            def hidden_hi(q):
                if q >= 2:
                    wait_used(act, D0 + q - 2)
                for c, f in runs(q):
                    last = cp(h_hi[:, q % 2, c[0]:c[1], :], hT[:, f[0]:f[1], :])
                last.then_inc(hs_hi, 1)

            for j in range(NPAIR):
                for u in range(2):
                    act.wait_ge(ff_ps, 4 * j + u + 1)
                    if j >= 2:
                        act.wait_ge(h_done, 2 * (j - 2) + u + 1)
                    nc.scalar.activation(silu_g[:, j % 2, u, :], ps[:, (0 if j % 2 else 4) + u, :], ACT.Silu
                                         ).then_inc(silu_done, 1)
                split_hi(G0 + 2 * j + 2)
                if j == NPAIR - 1:
                    for q in range(2):
                        hidden_hi(q)
                split_hi(G0 + 2 * j + 3)

            for q in range(2, NDOWN):
                split_hi(D0 + q)
                hidden_hi(q)
            for i in range(TILES):
                root(1, i)
                normalise(1, i)

        @block.vector
        def _(dve):
            V = nc.vector

            def split_lo(n):
                dve.wait_ge(hi_done, n + 1)
                size = size_of(n)
                V.tensor_tensor(w_lo[:, n % 2, 0:size], raw[:, n % 2, 0:size], w_hi[:, n % 2, 0:size].bitcast(F32),
                                ALU.subtract).then_inc(lo_done, 1)

            V.memset(eps_ln[:], LN_EPS)
            V.memset(eps_rms[:], RMS_EPS)
            dve.wait_ge(small_turned, 1)
            V.tensor_copy(small_t[:], ps[:, 3, 0:28]).then_inc(small_out, 1)
            dve.wait_ge(small_out, 1)
            V.tensor_tensor(lb_m[:], lb_l[:, 0, :], lb_l[:, 1, :], ALU.max).then_inc(lb_step, 1)
            dve.wait_ge(lb_step, 1)
            V.tensor_tensor(lb_e[:], lb_l, lb_m[:].unsqueeze(1).broadcast_to([P, 2, HG]), ALU.subtract).then_inc(lb_step, 1)
            dve.wait_ge(lb_exp, 1)
            V.tensor_tensor(lb_m[:], lb_e[:, 0, :], lb_e[:, 1, :], ALU.add).then_inc(lb_step, 1)
            dve.wait_ge(lb_step, 3)
            V.reciprocal(lb_m[:], lb_m[:]).then_inc(lb_step, 1)
            dve.wait_ge(lb_step, 4)
            V.tensor_tensor(lb[:], lb_e[:, 0, :], lb_m[:], ALU.mult).then_inc(lb_step, 1)
            dve.wait_ge(lb_step, 5)
            V.tensor_scalar(one_lb[:], lb[:], -1.0, 1.0, ALU.mult, ALU.add).then_inc(lb_step, 1)

            for kt in range(KT):
                dve.wait_ge(xT_hi_done, kt + 1)
                V.tensor_tensor(xT_lo[:, kt, :], ps[:, 4 + kt % 4, :], xT_hi[:, kt, :].bitcast(F32),
                                ALU.subtract).then_inc(xT_lo_done, 1)
                if kt == 4:
                    split_lo(0)
            split_lo(1)

            V.memset(mask[:, 0:P], 0.0).then_inc(mask_ready, 1)
            dve.wait_ge(mask_ready, 1)
            V.memset(mask[0:64, 64:P], FAR).then_inc(mask_ready, 1)

            def scores():
                dve.wait_ge(iw_ready, 1)
                for j in range(HEADS * len(TURN_TILES)):
                    h, i = j // 3, TURN_TILES[j % 3]
                    dve.wait_ge(rel_done, j + 1)
                    r, w = rel[:, j % 2, 0:P * (i + 1)], iw_n[:, i, h:h + 1]
                    if h == 0:
                        ins = V.tensor_scalar(sc(i), r, w, None, ALU.mult)
                    else:
                        dve.wait_ge(acc_done, j - 2)
                        ins = V.scalar_tensor_tensor(out=sc(i), in0=r, scalar=w, in1=sc(i), op0=ALU.mult, op1=ALU.add)
                    ins.then_inc(acc_done, 1)
                dve.wait_ge(acc_done, 24)
                for i in TURN_TILES:
                    V.memset(score[0:64, SC0[i] + P * i + 64:SC0[i] + P * (i + 1)], NEG).then_inc(acc_done, 1)
                dve.wait_ge(acc_done, 27)

            selected = [0]

            def select_keys(count):
                for k in range(selected[0], min(selected[0] + count, len(SELECT_STEPS))):
                    _, op, i = SELECT_STEPS[k]
                    if k >= 3:
                        dve.wait_ge(topk_step, k - 2)
                    if op == "max":
                        V.max(out=top8[:, i, :], in_=sc(i)).then_inc(topk_step, 1)
                    else:
                        V.match_replace(out=sc(i), in_to_replace=top8[:, i, :], in_values=sc(i),
                                        imm_value=TAKEN).then_inc(topk_step, 1)
                selected[0] += count

            def cumulate():
                for g in range(HG):
                    dve.wait_ge(ln_done, g + 1)
                    V.tensor_tensor_scan(out=GT[:, g, :], data0=keep_state[:], data1=GT[:, g, :], initial=0.0,
                                         op0=ALU.mult, op1=ALU.add).then_inc(G_done, 1)

            def keep_diagonal():
                dve.wait_ge(A_clear, 1)
                for h in range(HG):
                    dve.wait_ge(diag_ps, h + 1)
                    V.copy_predicated(out=AT[:, 4 * h:4 * h + 4, :],
                                      mask=ident[:].bitcast(I32).unsqueeze(1).broadcast_to([P, 4, P]),
                                      data=ps[:, (6, 7, 2, 3)[h], :].rearrange("p (a t) -> p a t", t=P)).then_inc(A_step, 1)

            def keep_level(l):
                m = LEVELS[l]
                for b in range(2):
                    dve.wait_ge(lev_ps, 2 * l + b + 1)
                    dve.wait_ge(A_step, 4 if l == 0 else 3 + 2 * l + b)
                    dst = AT[:, 8 * b:8 * b + 8, :].rearrange("p a (b t) -> p a b t", t=2 * m)[:, :, :, m:2 * m]
                    msk = level_mask[:, l, :].rearrange("p (b t) -> p b t", t=m).unsqueeze(1).broadcast_to([P, 8, CH // m, m])
                    src = ps[:, 2 + b, :].rearrange("p (a b t) -> p a b t", a=8, t=m)
                    V.copy_predicated(out=dst, mask=msk, data=src).then_inc(A_step, 1)

            def states(h0):
                dve.wait_ge(cd_exp, 1)
                dve.wait_ge(U_ps, h0 // 2 + 1)
                dve.wait_ge(kd_mul, 1)
                dve.wait_ge(qg_mul, 1)
                k = h0 * (NCH - 1)
                for c in range(NCH - 1):
                    for h in (h0, h0 + 1):
                        U = ps[:, (2, 6)[h % 2] + c % 2, (c // 2) * P:(c // 2 + 1) * P]
                        if c == 0:
                            ins = V.tensor_copy(state[:, h, c, :], U)
                        else:
                            dve.wait_ge(state_step, k - 1)
                            ins = V.scalar_tensor_tensor(out=state[:, h, c, :], in0=state[:, h, c - 1, :],
                                                         scalar=chunk_decay[:, h, c:c + 1], in1=U,
                                                         op0=ALU.mult, op1=ALU.add)
                        ins.then_inc(state_step, 1)
                        k += 1

            for j in range(NU):
                n, u, kind = UNITS[j]
                if u == 1 or kind == "ik":
                    split_lo(n + 2)
                if j == INDEX_AT:
                    dve.wait_ge(consts_ready, 1)
                    scores()
                if j > INDEX_AT:
                    select_keys(SELECT_A_UNIT)
                if j == FIRST["hq"] + 1:
                    cumulate()
                if j == DIAG_AT:
                    keep_diagonal()
                if j in LEVEL_AT:
                    keep_level(LEVEL_AT.index(j))
                if j in U_AT:
                    states(2 * U_AT.index(j))
            select_keys(len(SELECT_STEPS))
            dve.wait_ge(topk_step, len(SELECT_STEPS))
            for i in TURN_TILES:
                V.tensor_scalar(mask[:, M0[i]:M0[i] + P * (i + 1)], sc(i), TAKEN, FAR, ALU.not_equal,
                                ALU.mult).then_inc(mask_ready, 1)
            dve.wait_ge(mask_ready, 5)

            def bias(a):
                h, i = a // 4, a % 4
                n = P * (i + 1)
                pr = probs[:, a % NPROB, 0:n]
                dve.wait_ge(qk_done, a + 1)
                if a >= NPROB:
                    dve.wait_ge(pT_done, a - NPROB + 1)
                V.scalar_tensor_tensor(out=pr, in0=dist[:, 384 - P * i:384 - P * i + n], scalar=-(2.0 ** -(h + 1)),
                                       in1=ps[:, QK_BANKS[a % 4], 0:n], op0=ALU.mult, op1=ALU.add).then_inc(biased, 1)
                dve.wait_ge(biased, a + 1)
                V.tensor_tensor_reduce(out=pr, in0=pr, in1=mask[:, M0[i]:M0[i] + n], scale=-1.0, scalar=3.0e38,
                                       op0=ALU.add, op1=ALU.min, accum_out=nmax[:, a:a + 1]).then_inc(masked, 1)

            def inverse(a):
                dve.wait_ge(exp_done, a + 1)
                V.reciprocal(rinv[:, a:a + 1], rsum[:, a:a + 1]).then_inc(rinv_done, 1)

            def a_low(g):
                dve.wait_ge(a_hi_done, g + 1)
                V.tensor_tensor(xT_lo[:, g, :], ps[:, 2 + g % 2, :], xT_hi[:, g, :].bitcast(F32),
                                ALU.subtract).then_inc(a_lo_done, 1)

            def r_low(h):
                dve.wait_ge(r_hi, h + 1)
                V.tensor_tensor(xT_lo[:, 4 + h, :], hgT[:, h, :], xT_hi[:, 4 + h, :].bitcast(F32),
                                ALU.subtract).then_inc(r_lo, 1)

            def gate_r(h):
                dve.wait_ge(rms_done, h + 1)
                dve.wait_ge(o_out, h + 1)
                V.tensor_tensor(oT[:, h, :], oT[:, h, :], sq[:, h, :], ALU.mult).then_inc(r_a, 1)
                dve.wait_ge(r_a, h + 1)
                dve.wait_ge(hg_scaled, h + 1)
                V.tensor_tensor(hgT[:, h, :], oT[:, h, :], hgT[:, h, :], ALU.mult).then_inc(r_b, 1)

            bias(0)
            bias(1)
            for h in range(HG):
                dve.wait_ge(sq_done, h + 1)
                V.tensor_copy(oT[:, h, :], ps[:, 4 + h, :]).then_inc(o_out, 1)
            for s in range(2, STEPS + 2):
                inverse(s - 2)
                if s < STEPS:
                    bias(s)
                if s in (5, 6, 7, 8):
                    gate_r(s - 5)
                if s in (11, 12, 13, 14):
                    r_low(s - 11)
                if s - LAG - 12 in (0, 8, 16):
                    a_low((s - LAG - 12) // 8)
            a_low(3)
            split_lo(W0 + 2)
            split_lo(W0 + 3)

            def residual(s, i, half):
                c = slice(half * 512, half * 512 + 512)
                bank = ((4, 0) if s == 0 else (0, 4))[half] + i
                count = (2 * s + half) * TILES + i
                V.scalar_tensor_tensor(out=x1[:, i, c], in0=x1[:, i, c], scalar=ALPHA, in1=ps[:, bank, :],
                                       op0=ALU.mult, op1=ALU.add).then_inc(res_done, 1)
                dve.wait_ge(res_done, count + 1)
                return V.bn_stats(out=stats[:, s * TILES + i, half, :], in_=x1[:, i, c])

            def aggregate(s, i):
                k = s * TILES + i
                dve.wait_ge(ln_step, 2 * k + 1)
                V.bn_aggr(out=moments[:, k, :], in_=stats[:, k, :, :]).then_inc(ln_step, 1)

            def shift_of(s, i):
                k = s * TILES + i
                dve.wait_ge(ln_root, k + 1)
                V.reciprocal(spread[:, k:k + 1], spread[:, k:k + 1]).then_inc(ln_inv, 1)
                dve.wait_ge(ln_inv, k + 1)
                V.scalar_tensor_tensor(out=shift[:, k:k + 1], in0=moments[:, k, 0:1], scalar=-1.0,
                                       in1=spread[:, k:k + 1], op0=ALU.mult, op1=ALU.mult).then_inc(ln_shift, 1)

            for i in range(TILES):
                if i < TILES - 1:
                    dve.wait_ge(mix_half, i + 1)
                else:
                    dve.wait_ge(out_used, 2)
                dve.wait_ge(x1_loaded[i], 16)
                residual(0, i, 0)
            split_lo(G0)
            for i in range(TILES):
                dve.wait_ge(mix_done, i + 1)
                residual(0, i, 1).then_inc(ln_step, 1)
                aggregate(0, i)
                if i >= 1:
                    shift_of(0, i - 1)
            shift_of(0, TILES - 1)
            split_lo(G0 + 1)
            for kt in range(KT):
                dve.wait_ge(x1T_v_done, kt + 1)
                V.tensor_copy(xT_hi[:, kt, :], x1T_v[:, kt % 2, :]).then_inc(x1T_hi, 1)
                dve.wait_ge(x1T_hi, kt + 1)
                V.tensor_tensor(xT_lo[:, kt, :], x1T_v[:, kt % 2, :], xT_hi[:, kt, :].bitcast(F32),
                                ALU.subtract).then_inc(x1T_lo, 1)

            def hidden_lo(q):
                dve.wait_ge(hs_hi, q + 1)
                for c, f in runs(q):
                    last = V.tensor_tensor(h_lo[:, q % 2, c[0]:c[1], :], hT[:, f[0]:f[1], :],
                                           h_hi[:, q % 2, c[0]:c[1], :].bitcast(F32), ALU.subtract)
                last.then_inc(hs_lo, 1)

            for j in range(NPAIR):
                split_lo(G0 + 2 * j + 2)
                if j == NPAIR - 1:
                    for q in range(2):
                        hidden_lo(q)
                if j == 3:
                    dve.wait_ge(x1_g, TILES)
                for u in range(2):
                    dve.wait_ge(ff_ps, 4 * j + 3 + u)
                    dve.wait_ge(silu_done, 2 * j + u + 1)
                    V.tensor_tensor(hT[:, 2 * j + u, :], ps[:, (0 if j % 2 else 4) + 2 + u, :], silu_g[:, j % 2, u, :],
                                    ALU.mult).then_inc(h_done, 1)
                split_lo(G0 + 2 * j + 3)

            for q in range(2, NDOWN):
                split_lo(D0 + q)
                hidden_lo(q)
                if q == 7:
                    for i in range(TILES):
                        dve.wait_ge(down_done, i + 1)
                        dve.wait_ge(ln_b, i + 1)
                        residual(1, i, 0)

            def scale_g(i):
                dve.wait_ge(ln_norm, TILES + i + 1)
                V.tensor_tensor(x1[:, i, :], x1[:, i, :], g2[:], ALU.mult).then_inc(ln_g, 1)

            for i in range(TILES):
                dve.wait_ge(down_done, TILES + i + 1)
                residual(1, i, 1).then_inc(ln_step, 1)
                aggregate(1, i)
                if i >= 1:
                    shift_of(1, i - 1)
                if i >= 2:
                    scale_g(i - 2)
            shift_of(1, TILES - 1)
            scale_g(TILES - 2)
            scale_g(TILES - 1)

        @block.gpsimd
        def _(pool):
            g = nc.gpsimd
            n = [0]

            def then(ins):
                n[0] += 1
                ins.then_inc(const_step, 1)
                pool.wait_ge(const_step, n[0])

            then(g.memset(ident[:], 0.0))
            g.affine_select(out=ident[:], in_=ident[:], compare_op=ALU.not_equal, fill=1.0, base=0,
                            pattern=[[-1, P]], channel_multiplier=1).then_inc(ident_ready, 1)
            g.memset(mean_w[:], 1.0 / P)
            then(g.memset(keep_state[:], 1.0))
            then(g.iota(dist[:], pattern=[[-1, 512]], base=384, channel_multiplier=1,
                        allow_small_or_imprecise_dtypes=True))
            then(g.tensor_scalar(keep_state[:], dist[:], 0.0, None, ALU.max))
            then(g.tensor_scalar(dist[:], dist[:], -1.0, 0.0, ALU.mult, ALU.max))
            then(g.tensor_tensor(dist[:], dist[:], keep_state[:], ALU.add))
            then(g.memset(keep_state[:], 1.0))
            then(g.memset(keep_state[:].rearrange("p (c t) -> p c t", t=CH)[:, :, 0:1], 0.0))
            then(g.memset(level_mask[:], 1))
            for l, m in enumerate(LEVELS):
                v = level_mask[:, l, :].rearrange("p (b t) -> p b t", t=m)
                then(g.affine_select(out=v, in_=v, compare_op=ALU.is_ge, fill=0.0, base=0,
                                     pattern=[[-2 * m, CH // m], [0, m]], channel_multiplier=1))
                ins = g.affine_select(out=v, in_=v, compare_op=ALU.is_ge, fill=0.0, base=m - 1,
                                      pattern=[[2 * m, CH // m], [0, m]], channel_multiplier=-1)
                if l < len(LEVELS) - 1:
                    then(ins)
            ins.then_inc(consts_ready, 1)
            g.memset(AT[:], 0.0).then_inc(A_clear, 1)

            pool.wait_ge(lb_step, 6)
            for h in range(HG):
                pool.wait_ge(unit_out, FIRST["hf"] + h + 1)
                g.tensor_scalar(GT[:, h, :], kkT[:, h, :], one_lb[:, h:h + 1], lb[:, h:h + 1], ALU.mult,
                                ALU.add).then_inc(f_done, 1)
                pool.wait_ge(f_done, h + 1)
                g.tensor_scalar(kkT[:, h, :], GT[:, h, :], -1.0, 1.0, ALU.mult, ALU.add).then_inc(kk_done, 1)

            def halves(t, m):
                v = t[:].rearrange("p h (b t) -> p (h b) t", t=2 * m)
                return v[:, :, 0:m], v[:, :, m:2 * m]

            def sub(l):
                m = LEVELS[l]
                if l >= 2:
                    pool.wait_ge(lev_ps, 2 * (l - 1))
                G1, G2 = halves(GT, m)
                e1, e2 = halves(E1 if l % 2 else E0, m)
                ref = G1[:, :, m - 1:m].broadcast_to([P, HG * SEQ // (2 * m), m])
                g.tensor_tensor(e1, ref, G1, ALU.subtract).then_inc(lev_sub, 1)
                g.tensor_tensor(e2, G2, ref, ALU.subtract).then_inc(lev_sub, 1)

            def mul(l):
                m = LEVELS[l]
                pool.wait_ge(lev_exp, l + 1)
                e1, e2 = halves(E1 if l % 2 else E0, m)
                k1, _ = halves(kkT, m)
                _, q2 = halves(hqT, m)
                g.tensor_tensor(e1, e1, k1, ALU.mult).then_inc(lev_mul, 1)
                g.tensor_tensor(e2, e2, q2, ALU.mult).then_inc(lev_mul, 1)

            pool.wait_ge(G_done, HG)
            pool.wait_ge(acc_done, 24)
            sub(0)
            sub(1)
            pool.wait_ge(unit_out, FIRST["hq"] + HG)
            mul(0)
            mul(1)
            for l in range(2, len(LEVELS)):
                sub(l)
                mul(l)
            pool.wait_ge(lev_ps, 2 * (len(LEVELS) - 1))
            Gc = GT[:].rearrange("p h (c t) -> p (h c) t", t=CH)
            g.tensor_tensor(E0[:].rearrange("p h (c t) -> p (h c) t", t=CH),
                            Gc[:, :, CH - 1:CH].broadcast_to([P, HG * NCH, CH]), Gc, ALU.subtract).then_inc(kd_sub, 1)
            pool.wait_ge(kd_exp, 1)
            pool.wait_ge(diag_ps, HG)
            g.tensor_tensor(kkT[:], E0[:], kkT[:], ALU.mult).then_inc(kd_mul, 1)
            pool.wait_ge(qg_exp, 1)
            g.tensor_tensor(hqT[:], E1[:], hqT[:], ALU.mult).then_inc(qg_mul, 1)
            pool.wait_ge(small_out, 1)
            for h in range(HG):
                pool.wait_ge(unit_out, FIRST["hg"] + h + 1)
                g.tensor_scalar(hgT[:, h, :], hgT[:, h, :], norm_g[:, h:h + 1], None, ALU.mult
                                ).then_inc(hg_scaled, 1)

            for a in range(STEPS):
                pool.wait_ge(rinv_done, a + 1)
                if a == 0:
                    pool.wait_ge(o_ps, HG)
                if a >= 4:
                    pool.wait_ge(pT_done, a - 3)
                g.tensor_scalar(diag_inv[:, a % 4, :], ident[:], rinv[:, a:a + 1], None, ALU.mult).then_inc(diag_ready, 1)

            pool.wait_ge(par_loaded, 64)
            for i in range(TILES):
                pool.wait_ge(ln_norm, i + 1)
                g.tensor_tensor(x1[:, i, :], x1n[:, i, :], g1[:], ALU.mult).then_inc(x1_g, 1)
                pool.wait_ge(x1_g, i + 1)
                g.tensor_tensor(x1[:, i, :], x1[:, i, :], b1[:], ALU.add).then_inc(ln_b, 1)
            for i in range(TILES):
                pool.wait_ge(ln_g, i + 1)
                g.tensor_tensor(x1[:, i, :], x1[:, i, :], b2[:], ALU.add).then_inc(ln_b, 1)


_INS = ["x", "w_in", "w_out", "hg_lb_logits", "hg_norm_g", "ln1_g", "ln1_b", "w_gate", "w_up", "w_down",
        "ln2_g", "ln2_b"]


def kernel(**inputs):
    import numpy as np
    from concourse import bacc
    from concourse.bass_utils import run_bass_kernel_spmd

    nc = bacc.Bacc("TRN2", target_bir_lowering=False, num_devices=1)
    arrays, args = {}, []
    for name in _INS:
        a = np.ascontiguousarray(inputs[name])
        arrays[f"in_{name}"] = a
        args.append(nc.dram_tensor(f"in_{name}", a.shape, mybir.dt.from_np(a.dtype), kind="ExternalInput").ap())
    args.append(nc.dram_tensor("out_y", (1, SEQ, D), F32, kind="ExternalOutput").ap())
    build(nc, *args)
    return run_bass_kernel_spmd(nc, [arrays], core_ids=[0]).results[0]["out_y"]
```

```python
from contextlib import ExitStack

import concourse.bass as bass
from concourse import mybir

F32 = mybir.dt.float32
F32R = mybir.dt.float32r
I32 = mybir.dt.int32
ALU = mybir.AluOpType
ACT = mybir.ActivationFunctionType

P = 128
SEQ, D = 512, 1024
TILES = SEQ // P
KT = D // P
HEADS, DH = 8, 64
TOPK = 128
HG = 4
CH = 64
NCH = SEQ // CH
FF = 2816
FT = FF // P
ALPHA = 2.0 ** 0.25
LN_EPS, RMS_EPS = 1e-5, 1e-6
IDX_SCALE = (64 ** -0.5) * (8 ** -0.5)
NEG = -3.0e38
TAKEN = -3.4e38
FAR = -1.0e30
LEVELS = [32, 16, 8, 4, 2, 1]

IN_SLABS = [("iq", 1536, 256), ("iq", 1792, 256), ("ik", 2048, 72),
            ("hf", 2632, 256), ("hf", 2888, 256), ("hq", 2120, 256), ("hq", 2376, 256),
            ("hi", 3144, 256), ("hi", 3400, 256), ("hg", 3656, 256), ("hg", 3912, 256),
            ("dk", 512, 256), ("dk", 768, 256), ("dq", 0, 256), ("dq", 256, 256),
            ("dv", 1024, 256), ("dv", 1280, 256)]
N_IN = len(IN_SLABS)
OUT_SLABS = [(4, 0), (0, 0), (4, 1), (0, 1)]
W0 = N_IN
G0 = W0 + len(OUT_SLABS)
NPAIR = FT // 2
D0 = G0 + 2 * NPAIR
DOWN_ROWS = [(half, f) for half in range(2) for f in range(FT)]
NDOWN = len(DOWN_ROWS) // 4
SLOT_UP = (G0 + 1) % 2
UP_CAME = 16 * sum(1 for n in range(G0 + 2) if n % 2 == SLOT_UP)
LOOPS = (NPAIR - 3) // 2
assert NPAIR == 2 * LOOPS + 3

UNITS = [(n, u, kind) for n, (kind, _, w) in enumerate(IN_SLABS) for u in range(2 if w == 256 else 1)]
NU = len(UNITS)
FIRST = {kind: min(j for j, v in enumerate(UNITS) if v[2] == kind) for _, _, kind in UNITS}
INDEX_AT = FIRST["hf"]
TURN_TILES = (3, 2, 1)
SELECT_STEPS = [(r, op, i) for r in range(TOPK // 8) for op in ("max", "take") for i in TURN_TILES]
SELECT_A_UNIT = 4
DIAG_AT = 14
LEVEL_AT = [15 + 2 * l for l in range(len(LEVELS))]
KD_AT = 27
U_AT = [29, 31]
STEPS = HEADS * TILES
LAG = 6
ACT_LAG = 4
INV_LAG = 3
NPROB = 8
MIX_FROM = 33
QK_BANKS = (0, 1, 4, 5)
SETS = ((4, 5, 0, 1), (2, 3, 6, 7))


def build(nc, x, w_in, w_out, hg_lb_logits, hg_norm_g, ln1_g, ln1_b, w_gate, w_up, w_down,
          ln2_g, ln2_b, out):
    x_d = x.rearrange("a (i p) d -> p (a i) d", p=P)
    out_d = out.rearrange("a (i p) d -> p (a i) d", p=P)
    win_d = w_in.rearrange("a (k p) n -> p (a k) n", p=P)
    wout_d = w_out.rearrange("a (k p) n -> p (a k) n", p=P)
    gate_d = w_gate.rearrange("a (k p) n -> p (a k) n", p=P)
    up_d = w_up.rearrange("a (k p) n -> p (a k) n", p=P)
    down_d = w_down.rearrange("a (f p) n -> p (a f) n", p=P)

    with ExitStack() as ctx:
        def sem(name):
            return ctx.enter_context(nc.semaphore(name))

        top = [16512]

        def at(name, shape, dt, offset):
            return nc.alloc_sbuf_tensor_at(name, shape, dt, offset=offset)

        def keep(name, shape, dt=F32):
            size = 4
            for s in shape[1:]:
                size *= s
            t = at(name, shape, dt, top[0])
            top[0] += (size + 31) // 32 * 32
            assert top[0] <= 229344, (name, top[0])
            return t

        ctx.enter_context(nc.sbuf_tensor("arena", [P, 52000], F32))
        ident = keep("ident", [P, P])
        mean_w = keep("mean_w", [P, P])
        level_mask = keep("level_mask", [P, len(LEVELS), CH], I32)
        dist = keep("dist", [P, 512])
        keep_state = keep("keep_state", [P, 512])
        small = keep("small", [P, P])
        small_t = keep("small_t", [P, 28])
        lb_l = small_t[:, 0:8].rearrange("p (l h) -> p l h", h=HG)
        norm_g, g1_t, b1_t = small_t[:, 8:12], small_t[:, 12:20], small_t[:, 20:28]
        lb_e = keep("lb_e", [P, 2, HG])
        lb_m = keep("lb_m", [P, HG])
        lb = keep("lb", [P, HG])
        one_lb = keep("one_lb", [P, HG])
        iw_n = keep("iw_n", [P, TILES, HEADS])
        top8 = keep("top8", [P, TILES, 8])
        nmax = keep("nmax", [P, STEPS])
        rsum = keep("rsum", [P, STEPS])
        rinv = keep("rinv", [P, STEPS])
        chunk_decay = keep("chunk_decay", [P, HG, NCH])
        stats = keep("stats", [P, 2 * TILES, 2, 6])
        moments = keep("moments", [P, 2 * TILES, 2])
        spread = keep("spread", [P, 2 * TILES])
        shift = keep("shift", [P, 2 * TILES])
        eps_ln = keep("eps_ln", [P, 1])
        eps_rms = keep("eps_rms", [P, 1])

        xT_hi = keep("xT_hi", [P, KT, SEQ], F32R)
        xT_lo = keep("xT_lo", [P, KT, SEQ], F32R)
        w_hi = keep("w_hi", [P, 2, 2048], F32R)
        w_lo = keep("w_lo", [P, 2, 2048], F32R)
        raw = keep("raw", [P, 2, 2048])
        zone = top[0]
        hqT = keep("hqT", [P, HG, SEQ])
        hvN = keep("hvN", [P, TILES, 512])
        E0 = keep("E0", [P, HG, SEQ])
        E1 = keep("E1", [P, HG, SEQ])
        GT = keep("GT", [P, HG, SEQ])
        kkT = keep("kkT", [P, HG, SEQ])
        hgT = keep("hgT", [P, HG, SEQ])
        AT = keep("AT", [P, HG * TILES, P])
        kdN = keep("kdN", [P, HG * TILES, P])
        sq = keep("sq", [P, HG, SEQ])
        qT = keep("qT", [P, 4, SEQ])
        kT = keep("kT", [P, 4, SEQ])
        vN = keep("vN", [P, TILES, 512])
        SC0 = {1: 0, 2: 256, 3: 640}
        M0 = {0: 0, 1: 128, 2: 384, 3: 768}
        mask = keep("mask", [P, 1280])
        score = at("score", [P, 1152], F32, top[0])
        probs_a = keep("probs_a", [P, 5, SEQ])
        o = zone + 16384
        iq_hi = at("iq_hi", [P, 4, SEQ], F32R, o)
        iq_lo = at("iq_lo", [P, 4, SEQ], F32R, zone)
        ik_hi = at("ik_hi", [P, SEQ], F32R, o + 8192)
        ik_lo = at("ik_lo", [P, SEQ], F32R, zone + 8192)
        rel = at("rel", [P, 2, SEQ], F32, o + 10240)
        iwT = at("iwT", [P, SEQ], F32, o + 14336)
        state = at("state", [P, HG, NCH - 1, P], F32, o)
        probsT = at("probsT", [P, 2, TILES, SEQ], F32, zone + 32768)
        diag_inv = at("diag_inv", [P, 4, P], F32, zone + 57344)
        probs_b = at("probs_b", [P, 3, SEQ], F32, zone + 59392)
        oT = at("oT", [P, HG, SEQ], F32, zone + 65536)
        x_in = at("x_in", [P, TILES, D], F32, zone + 81920)
        x1 = at("x1", [P, TILES, D], F32, zone)
        g1 = at("g1", [P, D], F32, o)
        b1 = at("b1", [P, D], F32, o + 4096)
        g2 = at("g2", [P, D], F32, o + 8192)
        b2 = at("b2", [P, D], F32, o + 12288)
        x1T_v = at("x1T_v", [P, 2, SEQ], F32, zone + 32768)
        silu_g = at("silu_g", [P, 2, 2, SEQ], F32, zone + 32768)
        hT = at("hT", [P, FT, SEQ], F32, zone + 40960)
        o = zone + 40960 + FT * 2048
        x1n = at("x1n", [P, TILES, D], F32, o - 16384)
        h_hi = at("h_hi", [P, 2, 4, SEQ], F32R, o)
        h_lo = at("h_lo", [P, 2, 4, SEQ], F32R, o + 16384)
        assert o + 32768 <= 229344

        ps = ctx.enter_context(nc.psum_tensor("ps", [P, 8, 512], F32))

        x_loaded = [[sem(f"x_loaded{i}_{half}") for half in range(2)] for i in range(TILES)]
        first_loaded, first_hi, first_lo = sem("first_loaded"), sem("first_hi"), sem("first_lo")
        small_loaded, small_turned, small_out = sem("small_loaded"), sem("small_turned"), sem("small_out")
        raw_loaded = [sem(f"raw_loaded{i}") for i in range(2)]
        hi_done, lo_done = sem("hi_done"), sem("lo_done")
        out_used, down_used = sem("out_used"), sem("down_used")
        const_step, ident_ready, consts_ready = sem("const_step"), sem("ident_ready"), sem("consts_ready")
        xT_ps, xT_hi_done, xT_lo_done = sem("xT_ps"), sem("xT_hi_done"), sem("xT_lo_done")
        unit_done, unit_out = sem("unit_done"), sem("unit_out")
        iw_turned, iw_ready = sem("iw_turned"), sem("iw_ready")
        idx_split, idx_done, rel_done, acc_done = sem("idx_split"), sem("idx_done"), sem("rel_done"), sem("acc_done")
        topk_step, mask_ready = sem("topk_step"), sem("mask_ready")
        qk_done, biased, masked = sem("qk_done"), sem("biased"), sem("masked")
        exp_done, rinv_done, diag_ready = sem("exp_done"), sem("rinv_done"), sem("diag_ready")
        pT_done, pT_out = sem("pT_done"), sem("pT_out")
        pv_done, a_hi_done, a_lo_done = sem("pv_done"), sem("a_hi_done"), sem("a_lo_done")
        lb_step, lb_exp = sem("lb_step"), sem("lb_exp")
        f_done, kk_done, ln_done, G_done = sem("f_done"), sem("kk_done"), sem("ln_done"), sem("G_done")
        hg_scaled = sem("hg_scaled")
        A_clear, A_step = sem("A_clear"), sem("A_step")
        lev_sub, lev_exp, lev_mul, lev_ps = sem("lev_sub"), sem("lev_exp"), sem("lev_mul"), sem("lev_ps")
        diag_ps = sem("diag_ps")
        kd_sub, kd_exp, kd_mul = sem("kd_sub"), sem("kd_exp"), sem("kd_mul")
        kd_ps, kd_out = sem("kd_ps"), sem("kd_out")
        qg_exp, qg_mul, cd_exp = sem("qg_exp"), sem("qg_mul"), sem("cd_exp")
        U_ps, state_step = sem("U_ps"), sem("state_step")
        o_ps, o_out, sq_done, ms_ps, rms_ln, rms_done = (
            sem(s) for s in ("o_ps", "o_out", "sq_done", "ms_ps", "rms_ln", "rms_done"))
        r_a, r_b, r_hi, r_lo = sem("r_a"), sem("r_b"), sem("r_hi"), sem("r_lo")
        x1_loaded = [sem(f"x1_loaded{i}") for i in range(TILES)]
        par_loaded = sem("par_loaded")
        mix_done, res_done, ln_step, ln_root, ln_inv, ln_shift, ln_norm = (
            sem(s) for s in ("mix_done", "res_done", "ln_step", "ln_root", "ln_inv", "ln_shift", "ln_norm"))
        ln_g, ln_b, x1_g, mix_half = sem("ln_g"), sem("ln_b"), sem("x1_g"), sem("mix_half")
        x1T_ps, x1T_v_done, x1T_hi, x1T_lo = sem("x1T_ps"), sem("x1T_v_done"), sem("x1T_hi"), sem("x1T_lo")
        ff_ps, silu_done, h_done = sem("ff_ps"), sem("silu_done"), sem("h_done")
        hs_hi, hs_lo, down_done = sem("hs_hi"), sem("hs_lo"), sem("down_done")
        last_g, last_b, g_pool, stored = sem("last_g"), sem("last_b"), sem("g_pool"), sem("stored")

        block = ctx.enter_context(nc.Block())

        def size_of(n):
            return KT * IN_SLABS[n][2] if n < N_IN else 2048

        def wait_used(eng, n):
            if n < N_IN:
                eng.wait_ge(unit_done, sum(1 for m, _, _ in UNITS if m <= n))
            elif n < G0 - 1:
                eng.wait_ge(out_used, n - W0 + 1)
            elif n < G0:
                eng.wait_ge(mix_done, TILES)
            elif n < D0:
                eng.wait_ge(ff_ps, 2 * (n - G0) + 2)
            else:
                eng.wait_ge(down_used, n - D0 + 1)

        def probs(a, c0, c1):
            b = a % NPROB
            return probs_a[:, b, c0:c1] if b < 5 else probs_b[:, b - 5, c0:c1]

        def sc(i):
            return score[:, SC0[i]:SC0[i] + P * (i + 1)]

        def runs(q):
            half, f = DOWN_ROWS[4 * q]
            a = min(4, FT - f)
            return [((0, a), (f, f + a))] + ([((a, 4), (0, 4 - a))] if a < 4 else [])

        @block.sync
        def _(sp):
            def load(n, parts):
                if n >= 2:
                    sp.wait_ge(lo_done, n - 1)
                for dst, src in parts:
                    sp.dma_start(dst, src).then_inc(raw_loaded[n % 2], 16)

            def load_in(n):
                _, c, w = IN_SLABS[n]
                load(n, [(raw[:, n % 2, 0:KT * w].rearrange("p (k n) -> p k n", k=KT), win_d[:, :, c:c + w])])

            def load_out(q):
                k0, half = OUT_SLABS[q]
                load(W0 + q, [(raw[:, (W0 + q) % 2, :].rearrange("p (k n) -> p k n", k=4),
                               wout_d[:, k0:k0 + 4, half * 512:half * 512 + 512])])

            for half in range(2):
                c = slice(half * 512, half * 512 + 512)
                for i in range(TILES):
                    sp.dma_start(x_in[:, i, c], x_d[:, i, c]).then_inc(x_loaded[i][half], 16)
                sp.dma_start(raw[:, 0, half * 1024:half * 1024 + 1024].rearrange("p (k n) -> p k n", k=4),
                             win_d[:, 4 * half:4 * half + 4, IN_SLABS[0][1]:IN_SLABS[0][1] + 256]
                             ).then_inc(raw_loaded[0] if half else first_loaded, 16)
            for n in range(1, N_IN):
                load_in(n)
            load_out(0)
            load_out(1)
            sp.wait_ge(o_ps, HG)
            for i in range(TILES):
                sp.dma_start(x1[:, i, :], x_d[:, i, :]).then_inc(x1_loaded[i], 16)
            for t, v in ((g1, ln1_g), (b1, ln1_b), (g2, ln2_g), (b2, ln2_b)):
                sp.dma_start(t[:], v.partition_broadcast(P).rearrange("p a d -> p (a d)")).then_inc(par_loaded, 16)
            load_out(2)
            load_out(3)
            def load_pair(j):
                for v, w_d in enumerate((gate_d, up_d)):
                    slot = (G0 + v) % 2
                    sp.wait_ge(lo_done, 2 * j + (G0 + v - 1))
                    sp.dma_start(raw[:, slot, :].rearrange("p (k n) -> p k n", k=KT),
                                 w_d[:, :, bass.ds(256 * j, 256)]).then_inc(raw_loaded[slot], 16)

            load_pair(0)
            load_pair(1)
            with sp.Fori(0, LOOPS) as t:
                for jj in range(2):
                    load_pair(2 * t + (2 + jj))
            load_pair(NPAIR - 1)
            for q in range(NDOWN):
                n = D0 + q
                half, f = DOWN_ROWS[4 * q]
                v = raw[:, n % 2, :].rearrange("p (k n) -> p k n", k=4)
                a = min(4, FT - f)
                parts = [(v[:, 0:a, :], down_d[:, f:f + a, half * 512:half * 512 + 512])]
                if a < 4:
                    parts.append((v[:, a:4, :], down_d[:, 0:4 - a, 512:1024]))
                load(n, parts)
            for i, c, done, count in ((0, slice(0, D), ln_b, TILES + 1), (1, slice(0, D), ln_b, TILES + 2),
                                      (3, slice(0, 512), last_b, 1), (3, slice(512, D), last_b, 2),
                                      (2, slice(0, 512), ln_b, TILES + 3), (2, slice(512, D), last_b, 3)):
                sp.wait_ge(done, count)
                sp.dma_start(out_d[:, i, c], x1[:, i, c]).then_inc(stored, 16)
            sp.wait_ge(stored, 16 * 6)

        @block.tensor
        def _(pe):
            mm, turn = nc.tensor.matmul, nc.tensor.transpose

            def three(o, a_hi, a_lo, b_hi, b_lo, first, end):
                mm(o, a_hi, b_hi, start=first, stop=False)
                mm(o, a_hi, b_lo, start=False, stop=False)
                return mm(o, a_lo, b_hi, start=False, stop=end)

            def turn_x(kt):
                if kt >= 4:
                    pe.wait_ge(xT_lo_done, kt - 3)
                for i in range(TILES):
                    if kt % 4 == 0:
                        pe.wait_ge(x_loaded[i][kt // 4], 16)
                    last = turn(ps[:, 4 + kt % 4, i * P:(i + 1) * P], x_in[:, i, kt * P:(kt + 1) * P], ident[:])
                last.then_inc(xT_ps, 1)

            pe.wait_ge(ident_ready, 1)
            for kt in range(4):
                turn_x(kt)
            pe.wait_ge(small_loaded, 64)
            turn(ps[:, 3, 0:28], small[0:28, :], ident[0:28, 0:28]).then_inc(small_turned, 1)

            def part(o, slab, u, m, w, kt):
                c = kt * w + u * P
                return three(o, w_hi[:, slab, c:c + m], w_lo[:, slab, c:c + m], xT_hi[:, kt, :], xT_lo[:, kt, :],
                             kt == 0, kt == KT - 1)

            def product(o, slab, u, m, w, end_sem):
                for kt in range(KT):
                    last = part(o, slab, u, m, w, kt)
                last.then_inc(end_sem, 1)

            def first_unit():
                turn_x(4)
                turn_x(5)
                pe.wait_ge(first_lo, 1)
                for kt in range(KT):
                    pe.wait_ge(xT_lo_done, kt + 1)
                    if kt == 4:
                        pe.wait_ge(lo_done, 1)
                    last = part(ps[:, 0, :], 0, 0, P, 256, kt)
                    if kt < 2:
                        turn_x(kt + 6)
                last.then_inc(unit_done, 1)

            def unit(j):
                n, u, kind = UNITS[j]
                w = IN_SLABS[n][2]
                m = min(w, P)
                if u == 0:
                    pe.wait_ge(lo_done, n + 1)
                if j >= 2:
                    pe.wait_ge(unit_out, j - 1)
                if 2 <= j <= FIRST["ik"] + 2:
                    pe.wait_ge(idx_split, j - 1)
                if kind in ("hi", "dv"):
                    for half in range(2):
                        i = 2 * u + half
                        for kt in range(KT):
                            last = three(ps[:, j % 2, 256 * half:256 * half + 256], xT_hi[:, kt, i * P:(i + 1) * P],
                                         xT_lo[:, kt, i * P:(i + 1) * P], w_hi[:, n % 2, kt * 256:kt * 256 + 256],
                                         w_lo[:, n % 2, kt * 256:kt * 256 + 256], kt == 0, kt == KT - 1)
                    last.then_inc(unit_done, 1)
                else:
                    product(ps[0:m, j % 2, :], n % 2, u, m, w, unit_done)

            def index():
                pe.wait_ge(unit_out, FIRST["ik"] + 1)
                pe.wait_ge(idx_split, FIRST["ik"] + 1)
                for i in range(TILES):
                    last = turn(ps[:, 4, i * 8:i * 8 + 8], iwT[0:8, i * P:(i + 1) * P], ident[0:8, 0:8])
                last.then_inc(iw_turned, 1)
                for j in range(HEADS * len(TURN_TILES)):
                    h, i = j // 3, TURN_TILES[j % 3]
                    a = 64 * (h % 2)
                    if j >= 4:
                        pe.wait_ge(rel_done, j - 3)
                    q, k = (slice(a, a + 64), h // 2, slice(i * P, (i + 1) * P)), (slice(a, a + 64), slice(0, P * (i + 1)))
                    three(ps[:, SETS[1][j % 4], 0:P * (i + 1)], iq_hi[q], iq_lo[q], ik_hi[k], ik_lo[k],
                          True, True).then_inc(idx_done, 1)

            def pair(t, p):
                return t[:, p // 4, (p % 4) * P:(p % 4 + 1) * P]

            def diagonal():
                pe.wait_ge(unit_out, FIRST["hq"] + HG)
                pe.wait_ge(kk_done, HG)
                pe.wait_ge(rel_done, HEADS * len(TURN_TILES))
                for p in range(HG * TILES):
                    bank = (6, 7, 2, 3)[p // 4]
                    last = mm(ps[:, bank, (p % 4) * P:(p % 4 + 1) * P], pair(kkT, p), pair(hqT, p),
                              start=(p % 4 == 0), stop=(p % 4 == 3), skip_group_check=True)
                    if p % 4 == 3:
                        last.then_inc(diag_ps, 1)

            def level(l):
                m = LEVELS[l]
                pe.wait_ge(lev_mul, 2 * (l + 1))
                pe.wait_ge(A_step, 4 + 2 * l)
                for p in range(HG * TILES):
                    X = pair(E1 if l % 2 else E0, p)
                    second = X.rearrange("p (b t) -> p b t", t=2 * m)[:, :, m:2 * m]
                    o = ps[:, 2 + p // 8, (p % 8) * CH:(p % 8 + 1) * CH].rearrange("p (b t) -> p b t", t=m)
                    last = mm(o, X, second, start=(p % 8 == 0), stop=(p % 8 == 7), skip_group_check=True)
                    if p % 8 == 7:
                        last.then_inc(lev_ps, 1)

            def turn_kd():
                pe.wait_ge(kd_mul, 1)
                pe.wait_ge(A_step, 4 + 2 * len(LEVELS))
                for p in range(HG * TILES):
                    bank = (6, 7, 2, 3)[p // 4]
                    last = turn(ps[:, bank, (p % 4) * P:(p % 4 + 1) * P], pair(kkT, p), ident[:])
                    if p % 4 == 3:
                        last.then_inc(kd_ps, 1)

            def chunk_sums(h0):
                pe.wait_ge(kd_out, HG)
                if h0:
                    pe.wait_ge(state_step, 2 * (NCH - 1))
                pe.wait_ge(unit_out, FIRST["hi"] + HG)
                for h in (h0, h0 + 1):
                    for c in range(NCH - 1):
                        b, f = CH * (c % 2), (c // 2) * P
                        last = mm(ps[:, (2, 6)[h % 2] + c % 2, f:f + P], kdN[b:b + CH, 4 * h + c // 2, :],
                                  hvN[b:b + CH, c // 2, h * P:(h + 1) * P], start=(c < 2), stop=(c >= NCH - 3),
                                  skip_group_check=True)
                last.then_inc(U_ps, 1)

            def outputs():
                pe.wait_ge(qg_mul, 1)
                pe.wait_ge(state_step, 4 * (NCH - 1))
                for h in range(HG):
                    bank = 4 + h
                    for p in range(TILES):
                        mm(ps[:, bank, p * P:(p + 1) * P], hvN[:, p, h * P:(h + 1) * P], AT[:, 4 * h + p, :],
                           start=(p == 0), stop=False, skip_group_check=True)
                    for c in range(1, NCH):
                        last = mm(ps[:, bank, c * CH:(c + 1) * CH], state[:, h, c - 1, :], hqT[:, h, c * CH:(c + 1) * CH],
                                  start=False, stop=(c == NCH - 1), skip_group_check=True)
                    last.then_inc(o_ps, 1)

            first_unit()
            for j in range(NU):
                if j:
                    unit(j)
                if j == INDEX_AT:
                    index()
                if j == DIAG_AT:
                    diagonal()
                if j in LEVEL_AT:
                    level(LEVEL_AT.index(j))
                if j == KD_AT:
                    turn_kd()
                if j in U_AT:
                    chunk_sums(2 * U_AT.index(j))
            def qk(a):
                h, i = a // 4, a % 4
                b = 64 * (h % 2)
                if a == 0:
                    pe.wait_ge(unit_out, NU)
                if a in (2, 3):
                    pe.wait_ge(o_out, a - 1)
                if a >= 4:
                    pe.wait_ge(biased, a - 3)
                mm(ps[:, QK_BANKS[a % 4], 0:P * (i + 1)], qT[b:b + 64, h // 2, i * P:(i + 1) * P],
                   kT[b:b + 64, h // 2, 0:P * (i + 1)], start=True, stop=True).then_inc(qk_done, 1)

            def turn_p(a):
                i = a % 4
                pe.wait_ge(diag_ready, a + 1)
                if a == 0:
                    pe.wait_ge(rms_ln, HG)
                if a >= 2:
                    pe.wait_ge(pT_out, a - 1)
                for j in range(i + 1):
                    last = mm(ps[:, 6 + a % 2, j * P:(j + 1) * P], probs(a, j * P, (j + 1) * P),
                              diag_inv[:, a % 4, :], start=(j == 0), stop=(j == i), skip_group_check=True)
                last.then_inc(pT_done, 1)

            def pv(h):
                pe.wait_ge(pT_out, 4 * h + 4)
                g, b = h // 2, 64 * (h % 2)
                if h >= 4:
                    pe.wait_ge(a_lo_done, g - 1)
                for j in range(TILES):
                    last = mm(ps[b:b + 64, 2 + g % 2, j * P:SEQ], vN[:, j, h * DH:(h + 1) * DH],
                              probsT[:, h % 2, j, j * P:SEQ], start=(j == 0), stop=(j == TILES - 1))
                last.then_inc(pv_done, 1)

            def mix(q, rows=range(4)):
                n = W0 + q
                k0, half = OUT_SLABS[q]
                pe.wait_ge(lo_done, n + 1)
                order = [(kk, i) for kk in rows for i in range(TILES)]
                if q == 3:
                    order = [(kk, i) for i in range(TILES) for kk in range(4)]
                for kk, i in order:
                    c, r = slice(i * P, (i + 1) * P), slice(kk * 512, (kk + 1) * 512)
                    last = three(ps[:, SETS[half][i], :], xT_hi[:, k0 + kk, c], xT_lo[:, k0 + kk, c],
                                 w_hi[:, n % 2, r], w_lo[:, n % 2, r], k0 == 4 and kk == 0, k0 == 0 and kk == 3)
                    if q == 1 and kk == 3 and i < TILES - 1 or q == 3 and kk == 3:
                        last.then_inc(mix_half if q == 1 else mix_done, 1)
                if q < 3 and rows[-1] == 3:
                    last.then_inc(out_used, 1)

            qk(0)
            qk(1)
            outputs()
            qk(2)
            qk(3)
            for h in range(HG):
                pe.wait_ge(sq_done, h + 1)
                if h >= 2:
                    pe.wait_ge(o_out, h + 1)
                mm(ps[:, (2, 3, 6, 7)[h], :], mean_w[:], sq[:, h, :], start=True, stop=True).then_inc(ms_ps, 1)
            for s in range(4, STEPS + LAG):
                if s < STEPS:
                    qk(s)
                if s >= LAG:
                    turn_p(s - LAG)
                if s >= LAG + 5 and (s - LAG) % 4 == 1 and (s - LAG) // 4 <= HEADS - 1:
                    pv((s - LAG) // 4 - 1)
                if s in (MIX_FROM, MIX_FROM + 2):
                    if s == MIX_FROM:
                        pe.wait_ge(biased, STEPS)
                        pe.wait_ge(r_lo, HG)
                    mix(0, [(s - MIX_FROM) // 2])

            mix(0, [2])
            pv(HEADS - 1)
            mix(0, [3])
            pe.wait_ge(a_lo_done, 4)
            for q in (1, 2, 3):
                mix(q)

            def turn_x1(i, kt, last_of_kt):
                last = turn(ps[:, SETS[kt // 4][kt % 4], i * P:(i + 1) * P], x1n[:, i, kt * P:(kt + 1) * P], ident[:])
                if last_of_kt:
                    last.then_inc(x1T_ps, 1)

            for i in range(TILES - 1):
                pe.wait_ge(ln_norm, i + 1)
                for kt in range(4):
                    turn_x1(i, kt, False)
            for kt in range(4, 7):
                pe.wait_ge(res_done, TILES + kt - 3)
                for i in range(TILES - 1):
                    turn_x1(i, kt, False)
            pe.wait_ge(ln_norm, TILES)
            for kt in range(7):
                turn_x1(TILES - 1, kt, True)
            pe.wait_ge(res_done, 2 * TILES)
            for i in range(TILES):
                turn_x1(i, 7, i == TILES - 1)

            pe.wait_ge(lo_done, G0 + 1)
            for kt in range(KT):
                pe.wait_ge(x1T_lo, kt + 1)
                for b in range(min(kt + 1, 2)):
                    for k in (range(kt + 1) if b == kt else (kt,)):
                        last = part(ps[:, SETS[0][b], :], G0 % 2, b, P, 256, k)
                    if kt == KT - 1:
                        last.then_inc(ff_ps, 1)
            pe.wait_ge(lo_done, G0 + 2)
            for b in range(2):
                product(ps[:, SETS[0][2 + b], :], (G0 + 1) % 2, b, P, 256, ff_ps)

            def gate_up(j, jj, first=False):
                for v in range(2):
                    slot = (G0 + v) % 2
                    pe.wait_ge(lo_done, 2 * j + (G0 + v + 1))
                    if v == 0:
                        if first:
                            pe.wait_ge(x1T_lo, KT)
                        else:
                            pe.wait_ge(h_done, 2 * j - 2)
                    for u in range(2):
                        product(ps[:, SETS[jj][2 * v + u], :], slot, u, P, 256, ff_ps)

            gate_up(1, 1, first=True)
            with pe.Fori(0, LOOPS) as t:
                for jj in range(2):
                    gate_up(2 * t + (2 + jj), jj)
            gate_up(NPAIR - 1, 0)

            for q in range(NDOWN):
                n = D0 + q
                pe.wait_ge(lo_done, n + 1)
                pe.wait_ge(hs_lo, q + 1)
                if q == 0:
                    pe.wait_ge(h_done, 2 * NPAIR)
                order = [(kk, i) for kk in range(4) for i in range(TILES)]
                if q == NDOWN - 1:
                    order = [(kk, i) for i in range(TILES) for kk in range(4)]
                for kk, i in order:
                    half, f = DOWN_ROWS[4 * q + kk]
                    c, r = slice(i * P, (i + 1) * P), slice(kk * 512, (kk + 1) * 512)
                    last = three(ps[:, 4 * half + i, :], h_hi[:, q % 2, kk, c], h_lo[:, q % 2, kk, c],
                                 w_hi[:, n % 2, r], w_lo[:, n % 2, r], f == 0, f == FT - 1)
                    if f == FT - 1:
                        last.then_inc(down_done, 1)
                if q < NDOWN - 1:
                    last.then_inc(down_used, 1)

        @block.scalar
        def _(act):
            def cp(o, i, scale=1.0):
                return nc.scalar.activation(o, i, ACT.Copy, scale=scale)

            arrived = [0, 0]

            def split_hi(n):
                arrived[n % 2] += 32 if (n >= D0 and DOWN_ROWS[4 * (n - D0)][1] + 4 > FT) else 16
                act.wait_ge(raw_loaded[n % 2], arrived[n % 2])
                if n >= 2:
                    wait_used(act, n - 2)
                size = size_of(n)
                cp(w_hi[:, n % 2, 0:size], raw[:, n % 2, 0:size]).then_inc(hi_done, 1)

            act.dma_start(small[0:8, :], hg_lb_logits.rearrange("l (h k) -> (l h) k", k=P)).then_inc(small_loaded, 16)
            act.dma_start(small[8:12, :], hg_norm_g.rearrange("a (h v) -> (a h) v", v=P)).then_inc(small_loaded, 16)
            act.dma_start(small[12:20, :], ln1_g.rearrange("a (h v) -> (a h) v", v=P)).then_inc(small_loaded, 16)
            act.dma_start(small[20:28, :], ln1_b.rearrange("a (h v) -> (a h) v", v=P)).then_inc(small_loaded, 16)
            for kt in range(KT):
                act.wait_ge(xT_ps, kt + 1)
                cp(xT_hi[:, kt, :], ps[:, 4 + kt % 4, :]).then_inc(xT_hi_done, 1)
                if kt == 2:
                    act.wait_ge(first_loaded, 16)
                    cp(w_hi[:, 0, 0:1024], raw[:, 0, 0:1024]).then_inc(first_hi, 1)
                if kt == 5:
                    arrived[0] = 16
                    act.wait_ge(raw_loaded[0], 16)
                    cp(w_hi[:, 0, 1024:2048], raw[:, 0, 1024:2048]).then_inc(hi_done, 1)
            split_hi(1)
            act.wait_ge(lb_step, 2)
            nc.scalar.activation(lb_e[:], lb_e[:], ACT.Exp).then_inc(lb_exp, 1)

            def out_of(j):
                n, u, kind = UNITS[j]
                act.wait_ge(unit_done, j + 1)
                g = j - FIRST[kind]
                src = ps[:, j % 2, :]
                if kind == "iq":
                    cp(iq_hi[:, g, :], src).then_inc(unit_out, 1)
                elif kind == "ik":
                    cp(ik_hi[0:64, :], ps[0:64, j % 2, :])
                    cp(ik_hi[64:128, :], ps[0:64, j % 2, :])
                    cp(iwT[0:8, :], ps[64:72, j % 2, :]).then_inc(unit_out, 1)
                elif kind == "hf":
                    nc.scalar.activation(kkT[:, g, :], src, ACT.Sigmoid).then_inc(unit_out, 1)
                elif kind == "hq":
                    cp(hqT[:, g, :], src).then_inc(unit_out, 1)
                elif kind in ("hi", "dv"):
                    dst, c = (hvN if kind == "hi" else vN), 256 * (g // 2)
                    cp(dst[:, 2 * u:2 * u + 2, c:c + 256], src.rearrange("p (i f) -> p i f", i=2)).then_inc(unit_out, 1)
                elif kind == "hg":
                    nc.scalar.activation(hgT[:, g, :], src, ACT.Silu).then_inc(unit_out, 1)
                elif kind == "dk":
                    cp(kT[:, g, :], src).then_inc(unit_out, 1)
                else:
                    cp(qT[:, g, :], src, DH ** -0.5).then_inc(unit_out, 1)

            def relus():
                act.wait_ge(iw_turned, 1)
                cp(iw_n[:].rearrange("p i h -> p (i h)"), ps[:, 4, 0:32], IDX_SCALE).then_inc(iw_ready, 1)
                for j in range(HEADS * len(TURN_TILES)):
                    i = TURN_TILES[j % 3]
                    act.wait_ge(idx_done, j + 1)
                    if j >= 2:
                        act.wait_ge(acc_done, j - 1)
                    nc.scalar.activation(rel[:, j % 2, 0:P * (i + 1)], ps[:, SETS[1][j % 4], 0:P * (i + 1)],
                                         ACT.Relu).then_inc(rel_done, 1)

            def level_exp(l):
                e = E1 if l % 2 else E0
                act.wait_ge(lev_sub, 2 * (l + 1))
                nc.scalar.activation(e[:], e[:], ACT.Exp).then_inc(lev_exp, 1)

            def late_exps(part):
                if part == 0:
                    nc.scalar.activation(chunk_decay[:], GT[:].rearrange("p h (c t) -> p h c t", t=CH)[:, :, :, CH - 1],
                                         ACT.Exp).then_inc(cd_exp, 1)
                    act.wait_ge(kd_sub, 1)
                    nc.scalar.activation(E0[:], E0[:], ACT.Exp).then_inc(kd_exp, 1)
                else:
                    act.wait_ge(lev_ps, 2 * len(LEVELS))
                    nc.scalar.activation(E1[:], GT[:], ACT.Exp).then_inc(qg_exp, 1)

            def kd_turned():
                for h in range(HG):
                    act.wait_ge(kd_ps, h + 1)
                    cp(kdN[:, 4 * h:4 * h + 4, :], ps[:, (6, 7, 2, 3)[h], :].rearrange("p (a k) -> p a k", k=P)
                       ).then_inc(kd_out, 1)

            for j in range(NU):
                n, u, kind = UNITS[j]
                out_of(j)
                if j == INDEX_AT:
                    relus()
                if (u == 1 or kind == "ik") and j < NU - 1:
                    split_hi(n + 2)
                if j == FIRST["hq"]:
                    for g in range(HG):
                        act.wait_ge(kk_done, g + 1)
                        nc.scalar.activation(GT[:, g, :], GT[:, g, :], ACT.Ln).then_inc(ln_done, 1)
                if j + 3 in LEVEL_AT:
                    level_exp(LEVEL_AT.index(j + 3))
                if j == LEVEL_AT[-1]:
                    late_exps(0)
                if j == LEVEL_AT[-1] + 1:
                    late_exps(1)
                if j == KD_AT:
                    kd_turned()
            def exps(a):
                i = a % 4
                pr = probs(a, 0, P * (i + 1))
                act.wait_ge(masked, a + 1)
                nc.scalar.activation(pr, pr, ACT.Exp, bias=nmax[:, a:a + 1], scale=-1.0,
                                     accum_out=rsum[:, a:a + 1]).then_inc(exp_done, 1)

            def turned_p(a):
                h, i = a // 4, a % 4
                act.wait_ge(pT_done, a + 1)
                if a == 0:
                    act.wait_ge(qg_exp, 1)
                if h >= 2 and i == 0:
                    act.wait_ge(pv_done, h - 1)
                cp(probsT[:, h % 2, 0:i + 1, i * P:(i + 1) * P],
                   ps[:, 6 + a % 2, 0:P * (i + 1)].rearrange("p (j q) -> p j q", q=P)).then_inc(pT_out, 1)

            def a_high(g):
                act.wait_ge(pv_done, 2 * g + 2)
                cp(xT_hi[:, g, :], ps[:, 2 + g % 2, :]).then_inc(a_hi_done, 1)

            def r_high(h):
                act.wait_ge(r_b, h + 1)
                cp(xT_hi[:, 4 + h, :], hgT[:, h, :]).then_inc(r_hi, 1)

            for h in range(HG):
                act.wait_ge(o_ps, h + 1)
                nc.scalar.activation(sq[:, h, :], ps[:, 4 + h, :], ACT.Square).then_inc(sq_done, 1)
                if h < 2:
                    exps(h)
            for h in range(HG):
                act.wait_ge(ms_ps, h + 1)
                nc.scalar.activation(sq[:, h, :], ps[:, (2, 3, 6, 7)[h], :], ACT.Ln, bias=eps_rms[:, 0:1]).then_inc(rms_ln, 1)
            for s in range(2, STEPS + ACT_LAG):
                if s < STEPS:
                    exps(s)
                if 4 <= s < 4 + HG:
                    act.wait_ge(rms_ln, s - 3)
                    nc.scalar.activation(sq[:, s - 4, :], sq[:, s - 4, :], ACT.Exp, scale=-0.5).then_inc(rms_done, 1)
                if s >= ACT_LAG:
                    turned_p(s - ACT_LAG)
                if s in (17, 21, 25, 29):
                    r_high((s - 17) // 4)
                if s - ACT_LAG - 10 in (0, 8, 16):
                    a_high((s - ACT_LAG - 10) // 8)
            split_hi(W0 + 1)
            a_high(3)
            split_hi(W0 + 2)
            split_hi(W0 + 3)
            split_hi(G0)

            def root(s, i):
                k = s * TILES + i
                act.wait_ge(ln_step, 2 * k + 2)
                nc.scalar.activation(spread[:, k:k + 1], moments[:, k, 1:2], ACT.Sqrt, bias=eps_ln[:, 0:1]
                                     ).then_inc(ln_root, 1)

            def normalise(s, i):
                k = s * TILES + i
                act.wait_ge(ln_shift, k + 1)
                dst = x1n if s == 0 else x1
                nc.scalar.activation(dst[:, i, :], x1[:, i, :], ACT.Identity, scale=spread[:, k:k + 1],
                                     bias=shift[:, k:k + 1]).then_inc(ln_norm, 1)

            for i in range(TILES):
                root(0, i)
                normalise(0, i)
            for kt in range(KT):
                act.wait_ge(x1T_ps, kt + 1)
                if kt >= 2:
                    act.wait_ge(x1T_lo, kt - 1)
                nc.scalar.activation(x1T_v[:, kt % 2, :], ps[:, SETS[kt // 4][kt % 4], :], ACT.Identity,
                                     scale=g1_t[:, kt:kt + 1], bias=b1_t[:, kt:kt + 1]).then_inc(x1T_v_done, 1)

            def hidden_hi(q):
                if q >= 2:
                    wait_used(act, D0 + q - 2)
                for c, f in runs(q):
                    last = cp(h_hi[:, q % 2, c[0]:c[1], :], hT[:, f[0]:f[1], :])
                last.then_inc(hs_hi, 1)

            arrived[(G0 + 1) % 2] += 16
            came = list(arrived)

            def silus(j, jj, place_used=True):
                for u in range(2):
                    act.wait_ge(ff_ps, 4 * j + (u + 1))
                    if place_used:
                        act.wait_ge(h_done, 2 * j + (u - 3))
                    nc.scalar.activation(silu_g[:, jj, u, :], ps[:, SETS[jj][u], :], ACT.Silu
                                         ).then_inc(silu_done, 1)

            def split_next_hi(j):
                for v in range(2):
                    slot = (G0 + v) % 2
                    act.wait_ge(raw_loaded[slot], 16 * j + (came[slot] + 16))
                    act.wait_ge(ff_ps, 4 * j + (2 * v + 2))
                    cp(w_hi[:, slot, :], raw[:, slot, :]).then_inc(hi_done, 1)

            act.wait_ge(lo_done, G0 + 2)
            for j in range(2):
                silus(j, j, False)
                split_next_hi(j)
            with act.Fori(0, LOOPS) as t:
                for jj in range(2):
                    silus(2 * t + (2 + jj), jj)
                    split_next_hi(2 * t + (2 + jj))
            silus(NPAIR - 1, 0)
            for slot in range(2):
                arrived[slot] += 16 * (NPAIR - 1)
            split_hi(D0)
            for q in range(2):
                hidden_hi(q)
            split_hi(D0 + 1)

            for q in range(2, NDOWN):
                split_hi(D0 + q)
                hidden_hi(q)
            for i in range(TILES):
                root(1, i)
                if i < TILES - 1:
                    normalise(1, i)

        @block.vector
        def _(dve):
            V = nc.vector

            def split_lo(n):
                dve.wait_ge(hi_done, n + 1)
                size = size_of(n)
                V.tensor_tensor(w_lo[:, n % 2, 0:size], raw[:, n % 2, 0:size], w_hi[:, n % 2, 0:size].bitcast(F32),
                                ALU.subtract).then_inc(lo_done, 1)

            V.memset(eps_ln[:], LN_EPS)
            V.memset(eps_rms[:], RMS_EPS)
            for kt in range(KT):
                dve.wait_ge(xT_hi_done, kt + 1)
                V.tensor_tensor(xT_lo[:, kt, :], ps[:, 4 + kt % 4, :], xT_hi[:, kt, :].bitcast(F32),
                                ALU.subtract).then_inc(xT_lo_done, 1)
                if kt == 2:
                    dve.wait_ge(first_hi, 1)
                    V.tensor_tensor(w_lo[:, 0, 0:1024], raw[:, 0, 0:1024], w_hi[:, 0, 0:1024].bitcast(F32),
                                    ALU.subtract).then_inc(first_lo, 1)
                if kt == 5:
                    dve.wait_ge(hi_done, 1)
                    V.tensor_tensor(w_lo[:, 0, 1024:2048], raw[:, 0, 1024:2048], w_hi[:, 0, 1024:2048].bitcast(F32),
                                    ALU.subtract).then_inc(lo_done, 1)
            split_lo(1)
            dve.wait_ge(small_turned, 1)
            V.tensor_copy(small_t[:], ps[:, 3, 0:28]).then_inc(small_out, 1)
            dve.wait_ge(small_out, 1)
            V.tensor_tensor(lb_m[:], lb_l[:, 0, :], lb_l[:, 1, :], ALU.max).then_inc(lb_step, 1)
            dve.wait_ge(lb_step, 1)
            V.tensor_tensor(lb_e[:], lb_l, lb_m[:].unsqueeze(1).broadcast_to([P, 2, HG]), ALU.subtract).then_inc(lb_step, 1)
            dve.wait_ge(lb_exp, 1)
            V.tensor_tensor(lb_m[:], lb_e[:, 0, :], lb_e[:, 1, :], ALU.add).then_inc(lb_step, 1)
            dve.wait_ge(lb_step, 3)
            V.reciprocal(lb_m[:], lb_m[:]).then_inc(lb_step, 1)
            dve.wait_ge(lb_step, 4)
            V.tensor_tensor(lb[:], lb_e[:, 0, :], lb_m[:], ALU.mult).then_inc(lb_step, 1)
            dve.wait_ge(lb_step, 5)
            V.tensor_scalar(one_lb[:], lb[:], -1.0, 1.0, ALU.mult, ALU.add).then_inc(lb_step, 1)

            V.memset(mask[:, 0:P], 0.0).then_inc(mask_ready, 1)
            dve.wait_ge(mask_ready, 1)
            V.memset(mask[0:64, 64:P], FAR).then_inc(mask_ready, 1)

            def scores():
                dve.wait_ge(iw_ready, 1)
                for j in range(HEADS * len(TURN_TILES)):
                    h, i = j // 3, TURN_TILES[j % 3]
                    dve.wait_ge(rel_done, j + 1)
                    r, w = rel[:, j % 2, 0:P * (i + 1)], iw_n[:, i, h:h + 1]
                    if h == 0:
                        ins = V.tensor_scalar(sc(i), r, w, None, ALU.mult)
                    else:
                        dve.wait_ge(acc_done, j - 2)
                        ins = V.scalar_tensor_tensor(out=sc(i), in0=r, scalar=w, in1=sc(i), op0=ALU.mult, op1=ALU.add)
                    ins.then_inc(acc_done, 1)
                dve.wait_ge(acc_done, 24)
                for i in TURN_TILES:
                    V.memset(score[0:64, SC0[i] + P * i + 64:SC0[i] + P * (i + 1)], NEG).then_inc(acc_done, 1)
                dve.wait_ge(acc_done, 27)

            selected = [0]

            def select_keys(count):
                for k in range(selected[0], min(selected[0] + count, len(SELECT_STEPS))):
                    _, op, i = SELECT_STEPS[k]
                    if k >= 3:
                        dve.wait_ge(topk_step, k - 2)
                    if op == "max":
                        V.max(out=top8[:, i, :], in_=sc(i)).then_inc(topk_step, 1)
                    else:
                        V.match_replace(out=sc(i), in_to_replace=top8[:, i, :], in_values=sc(i),
                                        imm_value=TAKEN).then_inc(topk_step, 1)
                selected[0] += count

            def cumulate():
                for g in range(HG):
                    dve.wait_ge(ln_done, g + 1)
                    V.tensor_tensor_scan(out=GT[:, g, :], data0=keep_state[:], data1=GT[:, g, :], initial=0.0,
                                         op0=ALU.mult, op1=ALU.add).then_inc(G_done, 1)

            def keep_diagonal():
                dve.wait_ge(A_clear, 1)
                for h in range(HG):
                    dve.wait_ge(diag_ps, h + 1)
                    V.copy_predicated(out=AT[:, 4 * h:4 * h + 4, :],
                                      mask=ident[:].bitcast(I32).unsqueeze(1).broadcast_to([P, 4, P]),
                                      data=ps[:, (6, 7, 2, 3)[h], :].rearrange("p (a t) -> p a t", t=P)).then_inc(A_step, 1)

            def keep_level(l):
                m = LEVELS[l]
                for b in range(2):
                    dve.wait_ge(lev_ps, 2 * l + b + 1)
                    dve.wait_ge(A_step, 4 if l == 0 else 3 + 2 * l + b)
                    dst = AT[:, 8 * b:8 * b + 8, :].rearrange("p a (b t) -> p a b t", t=2 * m)[:, :, :, m:2 * m]
                    msk = level_mask[:, l, :].rearrange("p (b t) -> p b t", t=m).unsqueeze(1).broadcast_to([P, 8, CH // m, m])
                    src = ps[:, 2 + b, :].rearrange("p (a b t) -> p a b t", a=8, t=m)
                    V.copy_predicated(out=dst, mask=msk, data=src).then_inc(A_step, 1)

            def states(h0):
                dve.wait_ge(cd_exp, 1)
                dve.wait_ge(U_ps, h0 // 2 + 1)
                dve.wait_ge(kd_mul, 1)
                dve.wait_ge(qg_mul, 1)
                k = h0 * (NCH - 1)
                for c in range(NCH - 1):
                    for h in (h0, h0 + 1):
                        U = ps[:, (2, 6)[h % 2] + c % 2, (c // 2) * P:(c // 2 + 1) * P]
                        if c == 0:
                            ins = V.tensor_copy(state[:, h, c, :], U)
                        else:
                            dve.wait_ge(state_step, k - 1)
                            ins = V.scalar_tensor_tensor(out=state[:, h, c, :], in0=state[:, h, c - 1, :],
                                                         scalar=chunk_decay[:, h, c:c + 1], in1=U,
                                                         op0=ALU.mult, op1=ALU.add)
                        ins.then_inc(state_step, 1)
                        k += 1

            def index_lo(j):
                dve.wait_ge(unit_out, j + 1)
                if j < FIRST["ik"]:
                    V.tensor_tensor(iq_lo[:, j, :], ps[:, j % 2, :], iq_hi[:, j, :].bitcast(F32), ALU.subtract
                                    ).then_inc(idx_split, 1)
                else:
                    V.tensor_tensor(ik_lo[0:64, :], ps[0:64, j % 2, :], ik_hi[0:64, :].bitcast(F32), ALU.subtract)
                    V.tensor_tensor(ik_lo[64:128, :], ps[0:64, j % 2, :], ik_hi[0:64, :].bitcast(F32), ALU.subtract
                                    ).then_inc(idx_split, 1)

            for j in range(NU):
                n, u, kind = UNITS[j]
                if j <= FIRST["ik"]:
                    index_lo(j)
                if j == INDEX_AT:
                    dve.wait_ge(consts_ready, 1)
                    scores()
                if (u == 1 or kind == "ik") and j < NU - 1:
                    split_lo(n + 2)
                if j > INDEX_AT:
                    select_keys(SELECT_A_UNIT)
                if j == FIRST["hq"] + 1:
                    cumulate()
                if j == DIAG_AT:
                    keep_diagonal()
                if j in LEVEL_AT:
                    keep_level(LEVEL_AT.index(j))
                if j in U_AT:
                    states(2 * U_AT.index(j))
            select_keys(len(SELECT_STEPS))
            dve.wait_ge(topk_step, len(SELECT_STEPS))
            for i in TURN_TILES:
                V.tensor_scalar(mask[:, M0[i]:M0[i] + P * (i + 1)], sc(i), TAKEN, FAR, ALU.not_equal,
                                ALU.mult).then_inc(mask_ready, 1)
            dve.wait_ge(mask_ready, 5)
            def bias(a):
                h, i = a // 4, a % 4
                n = P * (i + 1)
                pr = probs(a, 0, n)
                dve.wait_ge(qk_done, a + 1)
                if a >= NPROB:
                    dve.wait_ge(pT_done, a - NPROB + 1)
                V.scalar_tensor_tensor(out=pr, in0=dist[:, 384 - P * i:384 - P * i + n], scalar=-(2.0 ** -(h + 1)),
                                       in1=ps[:, QK_BANKS[a % 4], 0:n], op0=ALU.mult, op1=ALU.add).then_inc(biased, 1)
                dve.wait_ge(biased, a + 1)
                V.tensor_tensor_reduce(out=pr, in0=pr, in1=mask[:, M0[i]:M0[i] + n], scale=-1.0, scalar=3.0e38,
                                       op0=ALU.add, op1=ALU.min, accum_out=nmax[:, a:a + 1]).then_inc(masked, 1)

            def inverse(a):
                dve.wait_ge(exp_done, a + 1)
                V.reciprocal(rinv[:, a:a + 1], rsum[:, a:a + 1]).then_inc(rinv_done, 1)

            def a_low(g):
                dve.wait_ge(a_hi_done, g + 1)
                V.tensor_tensor(xT_lo[:, g, :], ps[:, 2 + g % 2, :], xT_hi[:, g, :].bitcast(F32),
                                ALU.subtract).then_inc(a_lo_done, 1)

            def r_low(h):
                dve.wait_ge(r_hi, h + 1)
                V.tensor_tensor(xT_lo[:, 4 + h, :], hgT[:, h, :], xT_hi[:, 4 + h, :].bitcast(F32),
                                ALU.subtract).then_inc(r_lo, 1)

            bias(0)
            bias(1)
            for h in range(HG):
                dve.wait_ge(sq_done, h + 1)
                V.tensor_copy(oT[:, h, :], ps[:, 4 + h, :]).then_inc(o_out, 1)
                if h >= 2:
                    bias(h)
            inverse(0)
            for s in range(4, STEPS + INV_LAG):
                inverse(s - INV_LAG)
                if s < STEPS:
                    bias(s)
                if s in (19, 23, 27, 31):
                    r_low((s - 19) // 4)
                if s - LAG - 12 in (0, 8, 16):
                    a_low((s - LAG - 12) // 8)
            split_lo(W0 + 1)
            a_low(3)
            split_lo(W0 + 2)
            split_lo(W0 + 3)

            def residual(s, i, half):
                c = slice(half * 512, half * 512 + 512)
                bank = SETS[half][i] if s == 0 else 4 * half + i
                count = (2 * s + half) * TILES + i
                V.scalar_tensor_tensor(out=x1[:, i, c], in0=x1[:, i, c], scalar=ALPHA, in1=ps[:, bank, :],
                                       op0=ALU.mult, op1=ALU.add).then_inc(res_done, 1)
                dve.wait_ge(res_done, count + 1)
                return V.bn_stats(out=stats[:, s * TILES + i, half, :], in_=x1[:, i, c])

            def aggregate(s, i):
                k = s * TILES + i
                dve.wait_ge(ln_step, 2 * k + 1)
                V.bn_aggr(out=moments[:, k, :], in_=stats[:, k, :, :]).then_inc(ln_step, 1)

            def shift_of(s, i):
                k = s * TILES + i
                dve.wait_ge(ln_root, k + 1)
                V.reciprocal(spread[:, k:k + 1], spread[:, k:k + 1]).then_inc(ln_inv, 1)
                dve.wait_ge(ln_inv, k + 1)
                V.scalar_tensor_tensor(out=shift[:, k:k + 1], in0=moments[:, k, 0:1], scalar=-1.0,
                                       in1=spread[:, k:k + 1], op0=ALU.mult, op1=ALU.mult).then_inc(ln_shift, 1)

            for i in range(TILES):
                if i < TILES - 1:
                    dve.wait_ge(mix_half, i + 1)
                else:
                    dve.wait_ge(out_used, 2)
                dve.wait_ge(x1_loaded[i], 16)
                residual(0, i, 0)
            for i in range(TILES):
                dve.wait_ge(mix_done, i + 1)
                residual(0, i, 1).then_inc(ln_step, 1)
                aggregate(0, i)
                shift_of(0, i)
            for kt in range(KT):
                dve.wait_ge(x1T_v_done, kt + 1)
                V.tensor_copy(xT_hi[:, kt, :], x1T_v[:, kt % 2, :]).then_inc(x1T_hi, 1)
                dve.wait_ge(x1T_hi, kt + 1)
                V.tensor_tensor(xT_lo[:, kt, :], x1T_v[:, kt % 2, :], xT_hi[:, kt, :].bitcast(F32),
                                ALU.subtract).then_inc(x1T_lo, 1)

            def hidden_lo(q):
                dve.wait_ge(hs_hi, q + 1)
                for c, f in runs(q):
                    last = V.tensor_tensor(h_lo[:, q % 2, c[0]:c[1], :], hT[:, f[0]:f[1], :],
                                           h_hi[:, q % 2, c[0]:c[1], :].bitcast(F32), ALU.subtract)
                last.then_inc(hs_lo, 1)

            def split_next_lo(j, v):
                slot = (G0 + v) % 2
                dve.wait_ge(hi_done, 2 * j + (G0 + v + 3))
                V.tensor_tensor(w_lo[:, slot, :], raw[:, slot, :], w_hi[:, slot, :].bitcast(F32),
                                ALU.subtract).then_inc(lo_done, 1)

            def hidden(j, jj):
                for u in range(2):
                    dve.wait_ge(ff_ps, 4 * j + (3 + u))
                    dve.wait_ge(silu_done, 2 * j + (u + 1))
                    V.tensor_tensor(hT[:, bass.ds(2 * j + u, 1), :].rearrange("p a n -> p (a n)"),
                                    ps[:, SETS[jj][2 + u], :], silu_g[:, jj, u, :], ALU.mult).then_inc(h_done, 1)

            def pair_dve(j, jj):
                split_next_lo(j, 0)
                hidden(j, jj)
                split_next_lo(j, 1)

            pair_dve(0, 0)
            pair_dve(1, 1)
            dve.wait_ge(x1_g, TILES)
            with dve.Fori(0, LOOPS) as t:
                for jj in range(2):
                    pair_dve(2 * t + (2 + jj), jj)
            split_lo(D0)
            for q in range(2):
                hidden_lo(q)
            hidden(NPAIR - 1, 0)
            split_lo(D0 + 1)

            for q in range(2, NDOWN):
                split_lo(D0 + q)
                hidden_lo(q)
                if q == 7:
                    for i in range(TILES):
                        dve.wait_ge(down_done, i + 1)
                        dve.wait_ge(ln_b, i + 1)
                        residual(1, i, 0)

            def scale_g(i):
                dve.wait_ge(ln_norm, TILES + i + 1)
                V.tensor_tensor(x1[:, i, :], x1[:, i, :], g2[:], ALU.mult).then_inc(ln_g, 1)

            for i in range(TILES):
                dve.wait_ge(down_done, TILES + i + 1)
                residual(1, i, 1).then_inc(ln_step, 1)
                aggregate(1, i)
                if i < TILES - 1:
                    shift_of(1, i)
                if i in (1, 3):
                    scale_g(i - 1)
            k, i = 2 * TILES - 1, TILES - 1
            dve.wait_ge(ln_root, k + 1)
            V.reciprocal(spread[:, k:k + 1], spread[:, k:k + 1]).then_inc(ln_inv, 1)
            for half in range(2):
                c = slice(half * 512, half * 512 + 512)
                V.scalar_tensor_tensor(out=x1[:, i, c], in0=x1[:, i, c], scalar=moments[:, k, 0:1], in1=g2[:, c],
                                       op0=ALU.subtract, op1=ALU.mult).then_inc(last_g, 1)
            dve.wait_ge(ln_inv, k + 1)
            for half in range(2):
                c = slice(half * 512, half * 512 + 512)
                dve.wait_ge(last_g, half + 1)
                V.scalar_tensor_tensor(out=x1[:, i, c], in0=x1[:, i, c], scalar=spread[:, k:k + 1], in1=b2[:, c],
                                       op0=ALU.mult, op1=ALU.add).then_inc(last_b, 1)
            dve.wait_ge(ln_g, 2)
            V.tensor_tensor(x1[:, 2, 512:], x1[:, 2, 512:], b2[:, 512:], ALU.add).then_inc(last_b, 1)

        @block.gpsimd
        def _(pool):
            g = nc.gpsimd
            n = [0]

            def then(ins):
                n[0] += 1
                ins.then_inc(const_step, 1)
                pool.wait_ge(const_step, n[0])

            then(g.memset(ident[:], 0.0))
            g.affine_select(out=ident[:], in_=ident[:], compare_op=ALU.not_equal, fill=1.0, base=0,
                            pattern=[[-1, P]], channel_multiplier=1).then_inc(ident_ready, 1)
            g.memset(mean_w[:], 1.0 / P)
            then(g.memset(keep_state[:], 1.0))
            then(g.iota(dist[:], pattern=[[-1, 512]], base=384, channel_multiplier=1,
                        allow_small_or_imprecise_dtypes=True))
            then(g.tensor_scalar(keep_state[:], dist[:], 0.0, None, ALU.max))
            then(g.tensor_scalar(dist[:], dist[:], -1.0, 0.0, ALU.mult, ALU.max))
            then(g.tensor_tensor(dist[:], dist[:], keep_state[:], ALU.add))
            then(g.memset(keep_state[:], 1.0))
            then(g.memset(keep_state[:].rearrange("p (c t) -> p c t", t=CH)[:, :, 0:1], 0.0))
            then(g.memset(level_mask[:], 1))
            for l, m in enumerate(LEVELS):
                v = level_mask[:, l, :].rearrange("p (b t) -> p b t", t=m)
                then(g.affine_select(out=v, in_=v, compare_op=ALU.is_ge, fill=0.0, base=0,
                                     pattern=[[-2 * m, CH // m], [0, m]], channel_multiplier=1))
                ins = g.affine_select(out=v, in_=v, compare_op=ALU.is_ge, fill=0.0, base=m - 1,
                                      pattern=[[2 * m, CH // m], [0, m]], channel_multiplier=-1)
                if l < len(LEVELS) - 1:
                    then(ins)
            ins.then_inc(consts_ready, 1)
            g.memset(AT[:], 0.0).then_inc(A_clear, 1)

            pool.wait_ge(lb_step, 6)
            for h in range(HG):
                pool.wait_ge(unit_out, FIRST["hf"] + h + 1)
                g.tensor_scalar(GT[:, h, :], kkT[:, h, :], one_lb[:, h:h + 1], lb[:, h:h + 1], ALU.mult,
                                ALU.add).then_inc(f_done, 1)
                pool.wait_ge(f_done, h + 1)
                g.tensor_scalar(kkT[:, h, :], GT[:, h, :], -1.0, 1.0, ALU.mult, ALU.add).then_inc(kk_done, 1)

            def halves(t, m):
                v = t[:].rearrange("p h (b t) -> p (h b) t", t=2 * m)
                return v[:, :, 0:m], v[:, :, m:2 * m]

            def sub(l):
                m = LEVELS[l]
                if l >= 2:
                    pool.wait_ge(lev_ps, 2 * (l - 1))
                G1, G2 = halves(GT, m)
                e1, e2 = halves(E1 if l % 2 else E0, m)
                ref = G1[:, :, m - 1:m].broadcast_to([P, HG * SEQ // (2 * m), m])
                g.tensor_tensor(e1, ref, G1, ALU.subtract).then_inc(lev_sub, 1)
                g.tensor_tensor(e2, G2, ref, ALU.subtract).then_inc(lev_sub, 1)

            def mul(l):
                m = LEVELS[l]
                pool.wait_ge(lev_exp, l + 1)
                e1, e2 = halves(E1 if l % 2 else E0, m)
                k1, _ = halves(kkT, m)
                _, q2 = halves(hqT, m)
                g.tensor_tensor(e1, e1, k1, ALU.mult).then_inc(lev_mul, 1)
                g.tensor_tensor(e2, e2, q2, ALU.mult).then_inc(lev_mul, 1)

            pool.wait_ge(G_done, HG)
            pool.wait_ge(acc_done, 24)
            sub(0)
            sub(1)
            pool.wait_ge(unit_out, FIRST["hq"] + HG)
            mul(0)
            mul(1)
            for l in range(2, len(LEVELS)):
                sub(l)
                mul(l)
            pool.wait_ge(lev_ps, 2 * (len(LEVELS) - 1))
            Gc = GT[:].rearrange("p h (c t) -> p (h c) t", t=CH)
            g.tensor_tensor(E0[:].rearrange("p h (c t) -> p (h c) t", t=CH),
                            Gc[:, :, CH - 1:CH].broadcast_to([P, HG * NCH, CH]), Gc, ALU.subtract).then_inc(kd_sub, 1)
            pool.wait_ge(kd_exp, 1)
            pool.wait_ge(diag_ps, HG)
            g.tensor_tensor(kkT[:], E0[:], kkT[:], ALU.mult).then_inc(kd_mul, 1)
            pool.wait_ge(qg_exp, 1)
            g.tensor_tensor(hqT[:], E1[:], hqT[:], ALU.mult).then_inc(qg_mul, 1)
            pool.wait_ge(small_out, 1)
            for h in range(HG):
                pool.wait_ge(unit_out, FIRST["hg"] + h + 1)
                g.tensor_scalar(hgT[:, h, :], hgT[:, h, :], norm_g[:, h:h + 1], None, ALU.mult
                                ).then_inc(hg_scaled, 1)

            for a in range(STEPS):
                if a >= 10 and (a - 10) % 4 < 2 and (a - 10) // 4 < HG:
                    h = (a - 10) // 4
                    if a % 2 == 0:
                        pool.wait_ge(rms_done, h + 1)
                        pool.wait_ge(o_out, h + 1)
                        g.tensor_tensor(oT[:, h, :], oT[:, h, :], sq[:, h, :], ALU.mult).then_inc(r_a, 1)
                    else:
                        pool.wait_ge(r_a, h + 1)
                        pool.wait_ge(hg_scaled, h + 1)
                        g.tensor_tensor(hgT[:, h, :], oT[:, h, :], hgT[:, h, :], ALU.mult).then_inc(r_b, 1)
                pool.wait_ge(rinv_done, a + 1)
                if a == 0:
                    pool.wait_ge(o_ps, HG)
                if a >= 4:
                    pool.wait_ge(pT_done, a - 3)
                g.tensor_scalar(diag_inv[:, a % 4, :], ident[:], rinv[:, a:a + 1], None, ALU.mult).then_inc(diag_ready, 1)

            pool.wait_ge(hi_done, G0 + 1)
            pool.wait_ge(lo_done, G0)
            g.tensor_tensor(w_lo[:, G0 % 2, :], raw[:, G0 % 2, :], w_hi[:, G0 % 2, :].bitcast(F32), ALU.subtract
                            ).then_inc(lo_done, 1)
            pool.wait_ge(raw_loaded[SLOT_UP], UP_CAME)
            pool.wait_ge(mix_done, TILES)
            g.tensor_copy(w_hi[:, SLOT_UP, :], raw[:, SLOT_UP, :]).then_inc(hi_done, 1)
            pool.wait_ge(hi_done, G0 + 2)
            pool.wait_ge(lo_done, G0 + 1)
            g.tensor_tensor(w_lo[:, SLOT_UP, :], raw[:, SLOT_UP, :], w_hi[:, SLOT_UP, :].bitcast(F32), ALU.subtract
                            ).then_inc(lo_done, 1)
            pool.wait_ge(par_loaded, 64)
            for i in range(TILES):
                pool.wait_ge(ln_norm, i + 1)
                g.tensor_tensor(x1[:, i, :], x1n[:, i, :], g1[:], ALU.mult).then_inc(x1_g, 1)
                pool.wait_ge(x1_g, i + 1)
                g.tensor_tensor(x1[:, i, :], x1[:, i, :], b1[:], ALU.add).then_inc(ln_b, 1)
            def plus_b(i, c):
                g.tensor_tensor(x1[:, i, c], x1[:, i, c], b2[:, c], ALU.add).then_inc(ln_b, 1)

            pool.wait_ge(ln_g, 1)
            plus_b(0, slice(0, D))
            pool.wait_ge(ln_norm, TILES + 2)
            g.tensor_tensor(x1[:, 1, :], x1[:, 1, :], g2[:], ALU.mult).then_inc(g_pool, 1)
            pool.wait_ge(g_pool, 1)
            plus_b(1, slice(0, D))
            pool.wait_ge(ln_g, 2)
            plus_b(2, slice(0, 512))


_INS = ["x", "w_in", "w_out", "hg_lb_logits", "hg_norm_g", "ln1_g", "ln1_b", "w_gate", "w_up", "w_down",
        "ln2_g", "ln2_b"]


def kernel(**inputs):
    import numpy as np
    from concourse import bacc
    from concourse.bass_utils import run_bass_kernel_spmd

    nc = bacc.Bacc("TRN2", target_bir_lowering=False, num_devices=1)
    arrays, args = {}, []
    for name in _INS:
        a = np.ascontiguousarray(inputs[name])
        arrays[f"in_{name}"] = a
        args.append(nc.dram_tensor(f"in_{name}", a.shape, mybir.dt.from_np(a.dtype), kind="ExternalInput").ap())
    args.append(nc.dram_tensor("out_y", (1, SEQ, D), F32, kind="ExternalOutput").ap())
    build(nc, *args)
    return run_bass_kernel_spmd(nc, [arrays], core_ids=[0]).results[0]["out_y"]
```
